# Optimizing a Trainium2 kernel written in Bass

```python
import jax, jax.numpy as jnp
from jax import lax
import numpy as np

D_MODEL = 2048
BATCH = 1
SEQ = 512
DEPTH = 1

RET_HEADS = 8
RET_HEAD_DIM = D_MODEL // 16
RET_WIDTH = RET_HEADS * RET_HEAD_DIM
RET_CHUNK = 128
DSA_HEADS = 8
DSA_HEAD_DIM = D_MODEL // 16
DSA_WIDTH = DSA_HEADS * DSA_HEAD_DIM
IDX_HEADS = 16
IDX_DIM = 64
IDX_TOPK_MAX = 256
Q_BLOCK = 128
MEM_TOKENS = 256
MEM_HEADS = 4
MEM_HEAD_DIM = D_MODEL // 8
MEM_WIDTH = MEM_HEADS * MEM_HEAD_DIM
N_BRANCHES = 3
NEG_INF = -1e30
EPS = 1e-6

W_IN_SPLITS = (RET_WIDTH, RET_WIDTH, RET_WIDTH, RET_WIDTH,
               DSA_WIDTH, DSA_WIDTH, DSA_WIDTH, DSA_WIDTH,
               IDX_HEADS * IDX_DIM, IDX_DIM, IDX_HEADS,
               MEM_WIDTH, MEM_WIDTH,
               D_MODEL, D_MODEL, D_MODEL)
W_IN_COLS = sum(W_IN_SPLITS)

kernel_name = "hybrid_retention_dsa_memory_gated_block"

def rms_norm(x, w):
    xf = x.astype(jnp.float32)
    y = xf * lax.rsqrt(jnp.mean(xf * xf, axis=-1, keepdims=True) + EPS)
    return (y * w.astype(jnp.float32)).astype(x.dtype)

def alibi_slopes(n):
    return 2.0 ** (-8.0 * (jnp.arange(n, dtype=jnp.float32) + 1.0) / n)

def retention(q, k, v):
    B, H, L, dk = q.shape
    dv = v.shape[-1]
    C = RET_CHUNK
    N = L // C
    q, k, v = (t.astype(jnp.float32) for t in (q, k, v))
    log_g = jnp.log1p(-(2.0 ** (-5.0 - jnp.arange(H, dtype=jnp.float32))))
    idx = jnp.arange(C, dtype=jnp.float32)
    diff = idx[:, None] - idx[None, :]
    decay = jnp.where(diff >= 0, jnp.exp(log_g[:, None, None] * jnp.maximum(diff, 0.0)), 0.0)
    q_dec = jnp.exp(log_g[:, None] * (idx + 1.0))[None, :, :, None]
    k_dec = jnp.exp(log_g[:, None] * (C - 1.0 - idx))[None, :, :, None]
    chunk_dec = jnp.exp(log_g * C)[None, :, None, None]

    def to_chunks(t):
        return t.reshape(B, H, N, C, t.shape[-1]).transpose(2, 0, 1, 3, 4)

    def step(state, inp):
        qi, ki, vi = inp
        inner = jnp.einsum('bhid,bhjd->bhij', qi, ki) * decay[None]
        o = (jnp.einsum('bhij,bhjv->bhiv', inner, vi)
             + jnp.einsum('bhid,bhdv->bhiv', qi * q_dec, state))
        state = state * chunk_dec + jnp.einsum('bhjd,bhjv->bhdv', ki * k_dec, vi)
        return state, o

    s0 = jnp.zeros((B, H, dk, dv), jnp.float32)
    _, o = lax.scan(step, s0, (to_chunks(q), to_chunks(k), to_chunks(v)))
    return o.transpose(1, 2, 0, 3, 4).reshape(B, H, L, dv)

def head_group_norm(o, w):
    mu = jnp.mean(o, axis=-1, keepdims=True)
    var = jnp.mean(jnp.square(o - mu), axis=-1, keepdims=True)
    on = (o - mu) * lax.rsqrt(var + 1e-5)
    B, H, L, dv = o.shape
    return on.transpose(0, 2, 1, 3).reshape(B, L, H * dv) * w.astype(jnp.float32)

def dsa_attention(q, k, v, q_idx, k_idx, w_idx, top_k):
    B, L, H, D = q.shape
    nb = L // Q_BLOCK
    slopes = alibi_slopes(H)
    key_pos = jnp.arange(L)
    k_idx_f = k_idx.astype(jnp.float32)

    def blocks(t):
        return t.reshape((B, nb, Q_BLOCK) + t.shape[2:]).swapaxes(0, 1)

    def one_block(args):
        qb, qib, wb, qpos = args
        s = jnp.einsum('bqhe,bse->bqhs', qib.astype(jnp.float32), k_idx_f) * (IDX_DIM ** -0.5)
        score = jnp.einsum('bqh,bqhs->bqs', wb.astype(jnp.float32), jax.nn.relu(s))
        causal = key_pos[None, :] <= qpos[:, None]
        score = jnp.where(causal[None], score, NEG_INF)
        _, sel = lax.top_k(score, top_k)
        valid = sel <= qpos[None, :, None]
        k_sel = jax.vmap(lambda kb, ib: kb[ib])(k, sel)
        v_sel = jax.vmap(lambda vb, ib: vb[ib])(v, sel)
        logits = jnp.einsum('bqhd,bqkhd->bqhk', qb, k_sel).astype(jnp.float32) * (D ** -0.5)
        dist = (qpos[None, :, None] - sel).astype(jnp.float32)
        logits = logits - slopes[None, None, :, None] * dist[:, :, None, :]
        logits = jnp.where(valid[:, :, None, :], logits, NEG_INF)
        p = jax.nn.softmax(logits, axis=-1).astype(v.dtype)
        return jnp.einsum('bqhk,bqkhd->bqhd', p, v_sel)

    qpos_blocks = jnp.arange(L).reshape(nb, Q_BLOCK)
    out = lax.map(one_block, (blocks(q), blocks(q_idx), blocks(w_idx), qpos_blocks))
    return out.swapaxes(0, 1).reshape(B, L, H, D)

def memory_cross_attention(q, mem, mem_norm_w, w_mem_kv):
    B, L, _ = q.shape
    M = mem.shape[1]
    kv = rms_norm(mem, mem_norm_w) @ w_mem_kv
    km, vm = jnp.split(kv, 2, axis=-1)
    km = km.reshape(B, M, MEM_HEADS, MEM_HEAD_DIM)
    vm = vm.reshape(B, M, MEM_HEADS, MEM_HEAD_DIM)
    qh = q.reshape(B, L, MEM_HEADS, MEM_HEAD_DIM)
    logits = jnp.einsum('blhd,bmhd->bhlm', qh, km).astype(jnp.float32) * (MEM_HEAD_DIM ** -0.5)
    p = jax.nn.softmax(logits, axis=-1).astype(vm.dtype)
    return jnp.einsum('bhlm,bmhd->blhd', p, vm).reshape(B, L, MEM_WIDTH)

def hybrid_layer(x, mem, pre_norm_w, w_in, ret_gn_w, mem_norm_w, w_mem_kv,
                 w_up_ret, w_up_dsa, w_up_mem, w_o, post_norm_w):
    B, L, _ = x.shape
    top_k = min(IDX_TOPK_MAX, L // 4)
    h = rms_norm(x, pre_norm_w)
    z = h @ w_in
    points = np.cumsum(W_IN_SPLITS)[:-1].tolist()
    (rq, rk, rv, rg, aq, ak, av, ag, iq, ik, iw, mq, mg,
     g_ret, g_dsa, g_mem) = jnp.split(z, points, axis=-1)

    def heads_first(t, n):
        return t.reshape(B, L, n, -1).transpose(0, 2, 1, 3)
    o_ret = retention(heads_first(rq, RET_HEADS),
                      heads_first(rk, RET_HEADS) * (RET_HEAD_DIM ** -0.5),
                      heads_first(rv, RET_HEADS))
    y_ret = jax.nn.silu(rg) * head_group_norm(o_ret, ret_gn_w).astype(x.dtype)

    o_dsa = dsa_attention(aq.reshape(B, L, DSA_HEADS, DSA_HEAD_DIM),
                          ak.reshape(B, L, DSA_HEADS, DSA_HEAD_DIM),
                          av.reshape(B, L, DSA_HEADS, DSA_HEAD_DIM),
                          iq.reshape(B, L, IDX_HEADS, IDX_DIM), ik,
                          iw * (IDX_HEADS ** -0.5), top_k)
    y_dsa = jax.nn.silu(ag) * o_dsa.reshape(B, L, DSA_WIDTH)

    y_mem = jax.nn.silu(mg) * memory_cross_attention(mq, mem, mem_norm_w, w_mem_kv)

    merged = (jax.nn.sigmoid(g_ret) * (y_ret @ w_up_ret)
              + jax.nn.sigmoid(g_dsa) * (y_dsa @ w_up_dsa)
              + jax.nn.sigmoid(g_mem) * (y_mem @ w_up_mem))
    out = merged @ w_o
    return x + rms_norm(out, post_norm_w)

def setup_inputs(seed: int = 0) -> dict:
    key = jax.random.key(seed)
    ks = jax.random.split(key, 14)
    f32 = jnp.float32

    def nrm(k, shape, fan_in):
        return jax.random.normal(k, shape, f32) * (fan_in ** -0.5)

    def gain(k, shape):
        return 1.0 + 0.02 * jax.random.normal(k, shape, f32)

    return {
        "x": jax.random.normal(ks[0], (BATCH, SEQ, D_MODEL), f32),
        "mem": jax.random.normal(ks[1], (BATCH, MEM_TOKENS, D_MODEL), f32),
        "pre_norm_w": gain(ks[2], (DEPTH, D_MODEL)),
        "w_in": nrm(ks[3], (DEPTH, D_MODEL, W_IN_COLS), D_MODEL),
        "ret_gn_w": gain(ks[4], (DEPTH, RET_WIDTH)),
        "mem_norm_w": gain(ks[5], (DEPTH, D_MODEL)),
        "w_mem_kv": nrm(ks[6], (DEPTH, D_MODEL, 2 * MEM_WIDTH), D_MODEL),
        "w_up_ret": nrm(ks[7], (DEPTH, RET_WIDTH, D_MODEL), RET_WIDTH),
        "w_up_dsa": nrm(ks[8], (DEPTH, DSA_WIDTH, D_MODEL), DSA_WIDTH),
        "w_up_mem": nrm(ks[9], (DEPTH, MEM_WIDTH, D_MODEL), MEM_WIDTH),
        "w_o": nrm(ks[10], (DEPTH, D_MODEL, D_MODEL), D_MODEL),
        "post_norm_w": gain(ks[11], (DEPTH, D_MODEL)),
    }

def reference(x, mem, pre_norm_w, w_in, ret_gn_w, mem_norm_w, w_mem_kv,
              w_up_ret, w_up_dsa, w_up_mem, w_o, post_norm_w):
    for layer in range(DEPTH):
        x = hybrid_layer(x, mem, pre_norm_w[layer], w_in[layer], ret_gn_w[layer],
                         mem_norm_w[layer], w_mem_kv[layer], w_up_ret[layer],
                         w_up_dsa[layer], w_up_mem[layer], w_o[layer], post_norm_w[layer])
    return x


_drawn_inputs = setup_inputs


def setup_inputs(seed=0):
    import zlib

    import numpy as np

    out = dict(_drawn_inputs(seed))
    spreads = {}
    factors = {'ret_gn_w': 4.45, 'mem_norm_w': 8.0, 'post_norm_w': 4.112}
    for name, (base, spread) in spreads.items():
        noise = np.random.default_rng([zlib.crc32(name.encode()), seed]).standard_normal(out[name].shape)
        drawn = base * np.exp(spread * noise) if base else spread * noise
        out[name] = __import__('jax').numpy.asarray(drawn.astype(out[name].dtype))
    for name, factor in factors.items():
        out[name] = (out[name] * factor).astype(out[name].dtype)
    return out
```

```python
from contextlib import ExitStack

import numpy as np

import concourse.bass as bass
from concourse import mybir

F32 = mybir.dt.float32
F32R = mybir.dt.float32r
I32 = mybir.dt.int32
ALU = mybir.AluOpType
ACT = mybir.ActivationFunctionType
AX = mybir.AxisListType

P = 128
SEQ = 512
D = 2048
KT = D // P
TT = SEQ // P
MEM = 256
MT = MEM // P
HD = 128
WIDTH = 1024
NPAIR = WIDTH // 256
IDX_HEADS = 16
IDX_DIM = 64
TOPK = min(256, SEQ // 4)
MEM_HEADS = 4
MEM_HD = 256
GC = 256
EPS = 1e-6
GN_EPS = 1e-5
NEG = -1e30
TAKEN = -3e38
FAR = 1e32
RSQRT_SEED = float(0x5F3759DF)

RQ, RK, RV, RG, AQ, AK, AV, AG, IQ, IK = [WIDTH * n for n in range(10)]
IKW = IDX_DIM + IDX_HEADS
MQ = IK + IKW
MG = MQ + WIDTH
G_RET = MG + WIDTH
G_DSA = G_RET + D
G_MEM = G_DSA + D

ROW_AT = {0: 896, 1: 1024, 2: 512, 3: 0}
COL_AT = {0: 0, 1: 512, 2: 1024, 3: 896}
PACK = 1280

V_KV, V_MEM = 0, 64
V_UPM = V_MEM + 4 * 16
V_IKW = V_UPM + 8 * 12
V_RET = V_IKW + 8
V_UPR = V_RET + 4 * 40
V_DSA = V_UPR + 8 * 12
V_UPD = V_DSA + 4 * 32
V_OUT = V_UPD + 8 * 12
V_END = V_OUT + 4 * 16
N_KV, N_MEM, N_UPM, N_IKW, N_RET = 0, 8, 16, 32, 33
N_UPR = N_RET + 20
N_DSA = N_UPR + 16
N_UPD = N_DSA + 16
N_OUT = N_UPD + 16


def at_least(eng, sem, value):
    if isinstance(value, int) and value <= 0:
        return
    eng.wait_ge(sem, value)


class Steps:

    def __init__(self, eng, sem):
        self.eng, self.sem, self.base, self.n = eng, sem, 0, 0

    def then(self, ins):
        self.n += 1
        ins.then_inc(self.sem, 1)
        self.eng.wait_ge(self.sem, self.base + self.n)

    def enter(self, i, first, per):
        self.start = self.base + self.n
        self.base, self.n = self.start + (i - first) * per, 0

    def leave(self, turns, per):
        assert self.n == per, (self.n, per)
        self.base, self.n = self.start + turns * per, 0


def build(nc, x, mem, pre_norm_w, w_in, ret_gn_w, mem_norm_w, w_mem_kv, w_up_ret, w_up_dsa,
          w_up_mem, w_o, post_norm_w, out):
    with ExitStack() as ctx:
        base = 16640
        used = [base]

        def place(name, shape, dt=F32, at=None):
            size = 4 * int(np.prod(shape[1:]))
            if at is None:
                at = used[0]
                used[0] += (size + 31) // 32 * 32
            return nc.alloc_sbuf_tensor_at(name, shape, dt, offset=at), at

        def sem(name):
            return ctx.enter_context(nc.semaphore(name))

        h_hi, at_h = place("h_hi", [P, KT, SEQ], F32R)
        h_lo, at_hl = place("h_lo", [P, KT, SEQ], F32R)
        raw, _ = place("raw", [P, 4, 4, GC])
        w_hi, _ = place("w_hi", [P, 4, 2, GC], F32R)
        w_lo, _ = place("w_lo", [P, 4, 2, GC], F32R)
        y_hi, at_y = place("y_hi", [P, 8, SEQ], F32R)
        y_lo, _ = place("y_lo", [P, 8, SEQ], F32R)
        merged, at_m = place("merged", [P, KT, SEQ])
        z, at_z = place("z", [P, 8, SEQ])
        z_v = z[:, 6:8, :].rearrange("p a (t d) -> p (a t) d", t=4).rearrange(
            "p (t h) d -> p t h d", h=2)
        far, at_far = place("far", [P, TT, SEQ])
        iota_f, _ = place("iota_f", [P, SEQ])
        negtri, _ = place("negtri", [P, P])
        ident, _ = place("ident", [P, P])
        ones, _ = place("ones", [P, P])
        logg, _ = place("logg", [P, 8])
        slope, _ = place("slope", [P, 8])
        norm_w, _ = place("norm_w", [P, 40])
        stat, _ = place("stat", [P, 3, 8])
        top8, _ = place("top8", [P, 8])
        rmax, _ = place("rmax", [P, 2, 4])
        rsum, _ = place("rsum", [P, 2, 4])
        rinv, _ = place("rinv", [P, 2, 4])
        ssq, _ = place("ssq", [P, TT, 4])
        at_x = used[0]

        x_rows, _ = place("x_rows", [P, TT, D], at=at_m)
        mem_rows, _ = place("mem_rows", [P, MT, D], at=at_z)
        memt_hi, _ = place("memt_hi", [P, KT, MEM], F32R, at=at_y)
        memt_lo, _ = place("memt_lo", [P, KT, MEM], F32R, at=at_y + 16384)
        junk, _ = place("junk", [P, D], at=at_far)
        norm_rows, _ = place("norm_rows", [40, P], at=at_x)
        iota_i, _ = place("iota_i", [P, SEQ], I32, at=at_x + 512)
        km, _ = place("km", [P, 8, MEM], at=at_far)
        vm, _ = place("vm", [P, MT, WIDTH], at=at_x)
        p_mem, _ = place("p_mem", [P, TT, MEM], at=at_x + 8192)
        pt_mem, _ = place("pt_mem", [P, MT, SEQ], at=at_x + 12288)
        v_mem, _ = place("v_mem", [P, MT, MEM_HD], at=at_x + 16384)
        sm_a, _ = place("sm_a", [P, PACK], at=at_far)
        ikt, _ = place("ikt", [P, SEQ], at=at_far + 5120)
        iw, _ = place("iw", [P, TT, IDX_HEADS], at=at_far + 7168)
        score, _ = place("score", [P, TT, SEQ], at=at_x)
        sm_b, _ = place("sm_b", [P, PACK], at=at_x + 8192)
        iq, _ = place("iq", [P, 2, SEQ], at=at_x + 13312)
        decay, _ = place("decay", [P, SEQ], at=at_x + 17408)
        iwt, _ = place("iwt", [IDX_HEADS, SEQ], at=at_x + 17408)
        assert at_x + 17408 + 2048 <= nc.sbuf_usable_end, (at_x, nc.sbuf_usable_end)
        pr = [place("p_a", [P, PACK], at=at_x)[0], place("p_b", [P, PACK], at=at_x + 5120)[0]]
        pt = [place("pt_a", [P, PACK], at=at_x + 10240)[0], place("pt_b", [P, PACK], at=at_z)[0]]
        m_hi, _ = place("m_hi", [P, KT, SEQ], F32R, at=at_h)
        m_lo, _ = place("m_lo", [P, KT, SEQ], F32R, at=at_hl)
        o_rows, _ = place("o_rows", [P, TT, D], at=at_y)
        x_again, _ = place("x_again", [P, TT, D], at=at_m)
        post_w, _ = place("post_w", [P, D], at=at_far)
        sq_out, _ = place("sq_out", [P, 1024], at=at_x)
        sm = [sm_a, sm_b]

        ps = ctx.enter_context(nc.psum_tensor("ps", [P, 8, 512], F32))
        flat = ps[:, :, :].rearrange("p b n -> p (b n)")
        PACKED = 4 * 512

        raw_in = [sem(f"raw_in{i}") for i in range(4)]
        hi_ready, lo_ready, half_used = sem("hi_ready"), sem("lo_ready"), sem("half_used")
        z_done, sig_ready = sem("z_done"), sem("sig_ready")
        small_in, mem_in, x_in = sem("small_in"), sem("mem_in"), [sem(f"x_in{t}") for t in range(TT)]
        consts, pool_own = sem("consts"), sem("pool_own")
        sq_done, row_scaled, t_ready, t_hi, t_lo = (sem("sq_done"), sem("row_scaled"), sem("t_ready"),
                                                    sem("t_hi"), sem("t_lo"))
        norm_t, norm_ready = sem("norm_t"), sem("norm_ready")
        logit_full, logit_read, neg_max, exp_done, p_ready = (
            sem("logit_full"), sem("logit_read"), sem("neg_max"), sem("exp_done"), sem("p_ready"))
        pt_full, pt_ready, o_full, y_done, tanh_done = (
            sem("pt_full"), sem("pt_ready"), sem("o_full"), sem("y_done"), sem("tanh_done"))
        iwt_ready, iwt_full, iw_ready = sem("iwt_ready"), sem("iwt_full"), sem("iw_ready")
        idx_full, relu_done, relu_used = sem("idx_full"), sem("relu_done"), sem("relu_used")
        decay_ready, inner_full, inner_ready = sem("decay_ready"), sem("inner_full"), sem("inner_ready")
        ret_full, sq_ready, var_full, var_read = (sem("ret_full"), sem("sq_ready"), sem("var_full"),
                                                  sem("var_read"))
        m_hi_done, m_lo_done = sem("m_hi_done"), sem("m_lo_done")
        out_sq, out_done = sem("out_sq"), sem("out_done")
        again_in, post_in, final, stored, own = (sem("again_in"), sem("post_in"), sem("final"), sem("stored"),
                                                 sem("own"))

        def by_units(w):
            return w.rearrange("(u t p) n -> u p t n", t=4, p=P)

        win_u, wkv_u = by_units(w_in[0]), by_units(w_mem_kv[0])
        up_u = {"m": by_units(w_up_mem[0]), "r": by_units(w_up_ret[0]), "d": by_units(w_up_dsa[0])}
        wo_u = w_o[0].rearrange("(u t p) n -> u p t n", t=2, p=P)
        x_t = x[0].rearrange("(t p) d -> t p d", p=P)
        mem_t = mem[0].rearrange("(t p) d -> p t d", p=P)
        out_t = out[0].rearrange("(t p) d -> t p d", p=P)

        block = ctx.enter_context(nc.Block())

        @block.sync
        def _(sp):
            def unit(v, slot, src, cols=GC):
                at_least(sp, lo_ready, v - 6)
                sp.dma_start(raw[:, slot, :, 0:cols], src).then_inc(raw_in[slot], 16)

            def group(v, col, view=win_u, slot0=0, cols=GC):
                for u in range(4):
                    unit(v + 2 * u, (slot0 + u) % 4, view[u, :, :, bass.ds(col, cols)], cols)

            def two_units(v, col, view, slot0):
                at_least(sp, lo_ready, v + 2 - 6)
                for u in (1, 0):
                    sp.dma_start(raw[:, slot0 + u, :, :],
                                 view[u, :, :, bass.ds(col, GC)]).then_inc(raw_in[slot0 + u], 16)

            sp.dma_start(norm_rows[0:16, :], pre_norm_w[0].rearrange("(k p) -> k p", p=P)).then_inc(small_in, 16)
            sp.dma_start(norm_rows[16:32, :], mem_norm_w[0].rearrange("(k p) -> k p", p=P)).then_inc(small_in, 16)
            sp.dma_start(norm_rows[32:40, :], ret_gn_w[0].rearrange("(k p) -> k p", p=P)).then_inc(small_in, 16)
            sp.dma_start(mem_rows[:, :, :], mem_t).then_inc(mem_in, 16)
            for t in range(TT):
                sp.dma_start(x_rows[:, t, :], x_t[t]).then_inc(x_in[t], 16)

            group(V_KV, 0, wkv_u)
            with sp.Fori(1, 8) as g:
                group(V_KV + 8 * g, g * GC, wkv_u)
            with sp.Fori(0, MEM_HEADS) as h:
                group(V_MEM + 16 * h, MQ + GC * h)
                group(V_MEM + 8 + 16 * h, MG + GC * h)

            def up_phase(v0, gate_col, view):
                with sp.Fori(0, 4) as i:
                    for e in range(2):
                        v = v0 + 24 * i + 12 * e
                        group(v, gate_col + 2 * GC * i + GC * e, slot0=2 * e)
                        two_units(v + 8, 2 * GC * i + GC * e, view, 2 * e)

            up_phase(V_UPM, G_MEM, up_u["m"])
            group(V_IKW, IK, cols=IKW)
            with sp.Fori(0, NPAIR) as p:
                for n, part in enumerate((IQ, RK, RQ, RG, RV)):
                    v = V_RET + 8 * n + 40 * p
                    if part:
                        group(v, part + GC * p)
                    else:
                        two_units(v, part + GC * p, win_u, 0)
                        for u in (2, 3):
                            unit(v + 2 * u, u, win_u[u, :, :, bass.ds(part + GC * p, GC)])
            up_phase(V_UPR, G_RET, up_u["r"])
            with sp.Fori(0, NPAIR) as p:
                for n, part in enumerate((AK, AQ, AG, AV)):
                    group(V_DSA + 8 * n + 32 * p, part + GC * p)
            up_phase(V_UPD, G_DSA, up_u["d"])
            def out_group(g):
                for u in (1, 0, 2, 3, 4, 5, 6, 7):
                    if u > 0:
                        at_least(sp, lo_ready, V_OUT + 2 * u - 6 + 16 * g)
                    sp.dma_start(raw[:, u % 4, :, :].rearrange("p (t a) n -> p t (a n)", t=2),
                                 wo_u[u, :, :, bass.ds(512 * g, 512)]).then_inc(raw_in[u % 4], 16)
            out_group(0)
            sp.wait_ge(m_lo_done, KT)
            sp.dma_start(post_w[:, :], post_norm_w[0:1, :].broadcast_to([P, D])).then_inc(post_in, 16)
            sp.dma_start(x_again[:, :, :], x[0].rearrange("(t p) d -> p t d", p=P)).then_inc(again_in, 16)
            with sp.Fori(1, 4) as g:
                out_group(g)
            for t in range(TT):
                sp.wait_ge(final, t + 1)
                sp.dma_start(out_t[t], o_rows[:, t, :]).then_inc(stored, 16)
            sp.wait_ge(stored, 16 * TT)

        @block.gpsimd
        def _(pool):
            nc.gpsimd.memset(ident[:, :], 0.0).then_inc(pool_own, 1)
            nc.gpsimd.memset(ones[:, :], 1.0 / HD).then_inc(consts, 1)
            nc.gpsimd.iota(iota_i[:, :], pattern=[[1, SEQ]], base=0, channel_multiplier=-1).then_inc(pool_own, 1)
            pool.wait_ge(pool_own, 2)
            nc.gpsimd.affine_select(out=ident[:, :], in_=ident[:, :], compare_op=ALU.not_equal, fill=1.0,
                                    base=0, pattern=[[-1, P]], channel_multiplier=1).then_inc(consts, 1)
            nc.gpsimd.tensor_copy(iota_f[:, :], iota_i[:, :]).then_inc(consts, 1)
            for h in range(8):
                nc.gpsimd.memset(logg[:, h:h + 1], float(np.log1p(-(2.0 ** (-5.0 - h)))))
                nc.gpsimd.memset(slope[:, h:h + 1], -(2.0 ** (-(h + 1.0)))).then_inc(consts, 1)

            def lo(v, j, cols=GC):
                pool.wait_ge(hi_ready, v + 1)
                s = j % 4
                nc.gpsimd.tensor_tensor(w_lo[:, s, :, 0:cols],
                                        raw[:, (j // 2) % 4, 2 * (j % 2):2 * (j % 2) + 2, 0:cols],
                                        w_hi[:, s, :, 0:cols].bitcast(F32), ALU.subtract).then_inc(lo_ready, 1)

            with pool.Fori(0, (V_IKW - V_KV) // 8) as i:
                for j in range(8):
                    lo(V_KV + 8 * i + j, j)
            for j in range(8):
                lo(V_IKW + j, j, IKW)
            with pool.Fori(0, (V_END - V_RET) // 8) as i:
                for j in range(8):
                    lo(V_RET + 8 * i + j, j)

        @block.scalar
        def _(act):
            def hi(v, j, turn, cols=GC):
                slot = (j // 2) % 4
                act.wait_ge(raw_in[slot], 16 * turn + 16)
                at_least(act, half_used, v - 3)
                nc.scalar.activation(w_hi[:, j % 4, :, 0:cols],
                                     raw[:, slot, 2 * (j % 2):2 * (j % 2) + 2, 0:cols],
                                     ACT.Copy).then_inc(hi_ready, 1)

            def run(first, i, per, count, hooks):
                if isinstance(i, int):
                    v, turn = first + i * per, (first + i * per) // 8
                else:
                    v, turn = first + i * per, first // 8 + i * (per // 8)
                for k in range(count):
                    hi(v + k, k % 8, turn + k // 8)
                    for f in hooks.get(k, ()):
                        f()

            act.wait_ge(mem_in, 16)
            for t in range(MT):
                at_least(act, sq_done, t)
                nc.scalar.activation(junk[:, :], mem_rows[:, t, :], ACT.Square,
                                     accum_out=stat[:, 0, 4 + t:5 + t]).then_inc(sq_done, 1)
            for t in range(TT):
                act.wait_ge(x_in[t], 16)
                act.wait_ge(sq_done, MT + t)
                nc.scalar.activation(junk[:, :], x_rows[:, t, :], ACT.Square,
                                     accum_out=stat[:, 0, t:t + 1]).then_inc(sq_done, 1)
            act.wait_ge(norm_ready, 1)
            for n in range(2 * KT):
                k = n % KT
                act.wait_ge(t_ready, n + 1)
                dst, cols = (memt_hi, MEM) if n < KT else (h_hi, SEQ)
                col = k + (KT if n < KT else 0)
                nc.scalar.activation(dst[:, k, :], ps[:, n % 8, 0:cols], ACT.Copy,
                                     scale=norm_w[:, col:col + 1]).then_inc(t_hi, 1)

            run(V_KV, 0, 8, 8, {})
            with act.Fori(1, 8) as g:
                run(V_KV, g, 8, 8, {})

            def tanh_gate(bank, v):
                act.wait_ge(half_used, v)
                nc.scalar.activation(z[:, 4:6, :], ps[:, bank:bank + 2, :], ACT.Tanh,
                                     scale=0.5).then_inc(tanh_done, 1)

            def mem_turn(h, prev):
                def exps():
                    act.wait_ge(logit_read, h + 1)
                    softmax_exp_mem(h)
                hooks = {14: [exps]}
                if prev:
                    hooks[3] = [lambda: mem_tanh(h - 1)]
                run(V_MEM, h, 16, 16, hooks)

            def softmax_exp_mem(h):
                act.wait_ge(neg_max, h + 1)
                for b in range(TT):
                    ins = nc.scalar.activation(p_mem[:, b, :], p_mem[:, b, :], ACT.Exp,
                                               bias=rmax[:, 0, b:b + 1], accum_out=rsum[:, 0, b:b + 1])
                ins.then_inc(exp_done, 1)

            def mem_tanh(h):
                at_least(act, y_done, h)
                tanh_gate(2, V_MEM + 16 + 16 * h)

            mem_turn(0, False)
            with act.Fori(1, MEM_HEADS) as h:
                mem_turn(h, True)

            def up_phase(v0, g0, sig0, y_before, last_tanh):
                def turn(i, first):
                    def sig(e):
                        g = g0 + 4 * i + 2 * e
                        act.wait_ge(half_used, v0 + 8 + 12 * e + 24 * i)
                        act.wait_ge(z_done, g)
                        if first and e == 0:
                            act.wait_ge(y_done, y_before)
                        nc.scalar.activation(z[:, 0:2, :], ps[:, 0:2, :], ACT.Tanh,
                                             scale=0.5).then_inc(sig_ready, 1)
                    hooks = {11: [lambda: sig(0)], 23: [lambda: sig(1)]}
                    if first and last_tanh:
                        hooks[3] = [last_tanh]
                    run(v0, i, 24, 24, hooks)
                turn(0, True)
                with act.Fori(1, 4) as i:
                    turn(i, False)

            up_phase(V_UPM, N_UPM, 0, 4, lambda: mem_tanh(3))

            for j in range(8):
                hi(V_IKW + j, j, V_IKW // 8, IKW)

            def ret_turn(p):
                g0 = N_RET + 5 * p

                def relu(n):
                    act.wait_ge(idx_full, 4 * p + n + 1)
                    at_least(act, relu_used, 4 * p + n - 1)
                    if n < 2:
                        at_least(act, ret_full, 2 * p)
                    nc.scalar.activation(sm[n % 2][:, :], flat[:, PACKED:PACKED + PACK],
                                         ACT.Relu).then_inc(relu_done, 1)

                def decay_of(a):
                    at_least(act, inner_ready, 2 * p + a)
                    nc.scalar.activation(decay[:, :], iota_f[:, :], ACT.Exp,
                                         scale=logg[:, bass.ds(2 * p + a, 1)]).then_inc(decay_ready, 1)

                def tanh():
                    at_least(act, y_done, 4 + 2 * p)
                    tanh_gate(0, V_RET + 32 + 40 * p)
                run(V_RET, p, 40, 40, {16: [lambda: relu(0)], 18: [lambda: relu(1)], 20: [lambda: relu(2)],
                                       22: [lambda: relu(3)], 24: [lambda: decay_of(0)],
                                       31: [lambda: decay_of(1)], 35: [tanh]})

            ret_turn(0)
            with act.Fori(1, NPAIR) as p:
                ret_turn(p)
            up_phase(V_UPR, N_UPR, 8, 4 + 8, None)

            def dsa_turn(p):
                def exps(a):
                    act.wait_ge(neg_max, MEM_HEADS + 2 * p + a + 1)
                    for b in range(TT):
                        part = pr[a][:, ROW_AT[b]:ROW_AT[b] + P * (b + 1)]
                        ins = nc.scalar.activation(part, part, ACT.Exp, bias=rmax[:, a, b:b + 1],
                                                   accum_out=rsum[:, a, b:b + 1])
                    ins.then_inc(exp_done, 1)

                def tanh():
                    at_least(act, y_done, 12 + 2 * p)
                    tanh_gate(0, V_DSA + 24 + 32 * p)
                run(V_DSA, p, 32, 32, {23: [lambda: exps(0)], 26: [lambda: exps(1)], 27: [tanh]})

            dsa_turn(0)
            with act.Fori(1, NPAIR) as p:
                dsa_turn(p)
            up_phase(V_UPD, N_UPD, 16, 4 + 16, None)

            def m_split(k):
                act.wait_ge(z_done, N_OUT)
                nc.scalar.activation(m_hi[:, k, :], merged[:, k, :], ACT.Copy).then_inc(m_hi_done, 1)

            def out_squares(g):
                act.wait_ge(half_used, V_OUT + 16 * g + 16)
                for t in range(TT):
                    ins = nc.scalar.activation(sq_out[:, 0:512], ps[:, 4 * (g % 2) + t, :], ACT.Square,
                                               accum_out=ssq[:, t, g:g + 1])
                    ins.then_inc(out_sq, 1)
                    act.wait_ge(out_sq, 4 * g + t + 1)

            for k in range(KT // 4):
                m_split(k)
            first = {k: [lambda k=k: m_split(KT // 4 + k)] for k in range(3 * KT // 4)}
            run(V_OUT, 0, 16, 16, first)
            for g in range(1, 4):
                run(V_OUT, g, 16, 16, {4: [lambda: out_squares(g - 1)]})
            out_squares(3)

        @block.tensor
        def _(pe):
            def three(dst, w_at, m_hi_ap, m_lo_ap, first, last, skip=False):
                nc.tensor.matmul(dst, w_at(w_hi), m_hi_ap, start=first, stop=False, skip_group_check=skip)
                nc.tensor.matmul(dst, w_at(w_hi), m_lo_ap, start=False, stop=False, skip_group_check=skip)
                return nc.tensor.matmul(dst, w_at(w_lo), m_hi_ap, start=False, stop=last, skip_group_check=skip)

            def transposed(bank, count, rhs_hi, rhs_lo, cols=SEQ, m=P, tiles=2):
                def product(k, s):
                    for kk in range(2):
                        kt = 2 * k + kk
                        for i in range(tiles):
                            last = three(ps[0:m, bank + i, 0:cols],
                                         lambda w: w[:, s, kk, P * i:P * i + m],
                                         rhs_hi[:, kt, :], rhs_lo[:, kt, :], kt == 0, kt == 2 * count - 1)
                    return last
                return product

            def in_rows(bank, lhs_hi, lhs_lo, tiles, per_bank):
                def product(k, s):
                    for kk in range(2):
                        kt = 2 * k + kk
                        for t in range(tiles):
                            dst = ps[:, bank + t // per_bank, GC * (t % per_bank):GC * (t % per_bank) + GC]
                            tok = slice(P * t, P * t + P)
                            nc.tensor.matmul(dst, lhs_hi[:, kt, tok], w_hi[:, s, kk, :],
                                             start=(kt == 0 and t % per_bank == 0), stop=False,
                                             skip_group_check=True)
                            nc.tensor.matmul(dst, lhs_lo[:, kt, tok], w_hi[:, s, kk, :],
                                             start=False, stop=False, skip_group_check=True)
                            last = nc.tensor.matmul(dst, lhs_hi[:, kt, tok], w_lo[:, s, kk, :],
                                                    start=False, stop=kt == KT - 1, skip_group_check=True)
                    return last
                return product

            def group(v, g, product, hooks={}, at=0, count=8, banks_free=True):
                if banks_free:
                    at_least(pe, z_done, g - 1)
                for k in range(count):
                    pe.wait_ge(lo_ready, v + k + 1)
                    last = product(k, (at + k) % 4)
                    last.then_inc(half_used, 1)
                    for f in hooks.get(at + k, ()):
                        f()

            pe.wait_ge(small_in, 48)
            pe.wait_ge(consts, 11)
            nc.tensor.transpose(ps[:, 7, 0:40], norm_rows[0:40, :], ident[0:40, 0:40]).then_inc(norm_t, 1)
            for n in range(2 * KT):
                k = n % KT
                rows, tiles = (mem_rows, MT) if n < KT else (x_rows, TT)
                pe.wait_ge(row_scaled, MT if n < KT else MT + TT)
                if n >= 7:
                    pe.wait_ge(norm_ready, 1)
                at_least(pe, t_lo, n - 7)
                for t in range(tiles):
                    last = nc.tensor.transpose(ps[:, n % 8, P * t:P * t + P],
                                               rows[:, t, P * k:P * k + P], ident[:, :])
                last.then_inc(t_ready, 1)

            pe.wait_ge(t_lo, 2 * KT)
            group(V_KV, N_KV, transposed(0, 8, memt_hi, memt_lo, MEM))
            group(V_KV + 8, N_KV + 1, transposed(2, 8, memt_hi, memt_lo, MEM))
            with pe.Fori(1, 2) as i:
                for e in range(2):
                    group(V_KV + 16 * i + 8 * e, N_KV + 2 * i + e, transposed(2 * e, 8, memt_hi, memt_lo, MEM))
            with pe.Fori(2, 4) as i:
                for e in range(2):
                    group(V_KV + 16 * i + 8 * e, N_KV + 2 * i + e, in_rows(2 * e, memt_hi, memt_lo, MT, 1))

            proj = lambda bank: transposed(bank, 8, h_hi, h_lo)

            def mem_logits(h):
                pe.wait_ge(z_done, N_MEM + 2 * h + 1)
                at_least(pe, y_done, h)
                for t in range(TT):
                    for c in range(2):
                        last = nc.tensor.matmul(ps[:, 4 + t // 2, MEM * (t % 2):MEM * (t % 2) + MEM],
                                                z[:, 2 + c, P * t:P * t + P], km[:, bass.ds(2 * h + c, 1), :]
                                                .rearrange("p a m -> p (a m)"), start=c == 0, stop=c == 1)
                last.then_inc(logit_full, 1)

            def mem_turn_over(h):
                pe.wait_ge(p_ready, h + 1)
                at_least(pe, pt_ready, h)
                for t in range(TT):
                    for m in range(MT):
                        last = nc.tensor.transpose(ps[:, 6 + m, P * t:P * t + P],
                                                   p_mem[:, t, P * m:P * m + P], ident[:, :])
                last.then_inc(pt_full, 1)

            def mem_out(h):
                pe.wait_ge(pt_ready, h + 1)
                for c in range(2):
                    for m in range(MT):
                        last = nc.tensor.matmul(ps[:, 4 + c, :], v_mem[:, m, P * c:P * c + P],
                                                pt_mem[:, m, :], start=m == 0, stop=m == MT - 1)
                last.then_inc(o_full, 1)

            def mem_turn(h, prev):
                hooks = {0: [lambda: mem_turn_over(h - 1)], 3: [lambda: mem_out(h - 1)]} if prev else {}
                group(V_MEM + 16 * h, N_MEM + 2 * h, proj(0), hooks)
                group(V_MEM + 16 * h + 8, N_MEM + 2 * h + 1, proj(2), {1: [lambda: mem_logits(h)]})

            mem_turn(0, False)
            with pe.Fori(1, MEM_HEADS) as h:
                mem_turn(h, True)

            def up_phase(v0, g0, sig0, y_all, hooks):
                def up_product(k, s):
                    for kk in range(2):
                        kt = 2 * k + kk
                        for i in range(2):
                            last = three(ps[:, 2 + i, :], lambda w: w[:, s, kk, P * i:P * i + P],
                                         y_hi[:, kt, :], y_lo[:, kt, :], kt == 0, kt == 7)
                    return last

                def turn(i, first):
                    for e in range(2):
                        g = g0 + 4 * i + 2 * e
                        v = v0 + 24 * i + 12 * e
                        start = first and e == 0
                        if start:
                            pe.wait_ge(z_done, g - 1)
                        at_least(pe, sig_ready, sig0 + 2 * i + e)
                        group(v, g, proj(0), hooks if start else {}, banks_free=False)
                        if start:
                            pe.wait_ge(y_done, y_all)
                        group(v + 8, g + 1, up_product, count=4)
                turn(0, True)
                with pe.Fori(1, 4) as i:
                    turn(i, False)

            up_phase(V_UPM, N_UPM, 0, 4, {0: [lambda: mem_turn_over(3)], 3: [lambda: mem_out(3)]})

            pe.wait_ge(sig_ready, 8)
            pe.wait_ge(z_done, N_IKW)

            def ikw_product(k, s):
                for kk in range(2):
                    kt = 2 * k + kk
                    last = three(ps[0:IKW, 6, :], lambda w: w[:, s, kk, 0:IKW], h_hi[:, kt, :], h_lo[:, kt, :],
                                 kt == 0, kt == KT - 1)
                return last
            group(V_IKW, N_IKW, ikw_product)

            def iw_turn_over():
                pe.wait_ge(iwt_ready, 1)
                for t in range(TT):
                    last = nc.tensor.transpose(ps[:, 4, IDX_HEADS * t:IDX_HEADS * t + IDX_HEADS],
                                               iwt[:, P * t:P * t + P], ident[0:IDX_HEADS, 0:IDX_HEADS])
                last.then_inc(iwt_full, 1)

            def idx_scores(p, n):
                pe.wait_ge(z_done, N_RET + 5 * p + 1)
                if n == 0:
                    pe.wait_ge(iw_ready, 1)
                    at_least(pe, var_read, p)
                    at_least(pe, inner_ready, 2 * p)
                at_least(pe, relu_done, 4 * p + n)
                half = slice(IDX_DIM * (n % 2), IDX_DIM * (n % 2) + IDX_DIM)
                for b in range(TT):
                    w = P * (b + 1)
                    last = nc.tensor.matmul(flat[:, PACKED + ROW_AT[b]:PACKED + ROW_AT[b] + w],
                                            iq[half, n // 2, P * b:P * b + P], ikt[half, 0:w],
                                            start=True, stop=True)
                last.then_inc(idx_full, 1)

            def inner(p, a):
                pe.wait_ge(z_done, N_RET + 5 * p + 3)
                pe.wait_ge(relu_done, 4 * p + 4)
                at_least(pe, inner_ready, 2 * p + a)
                for j in range(TT):
                    last = nc.tensor.matmul(flat[:, PACKED + COL_AT[j]:PACKED + COL_AT[j] + SEQ - P * j],
                                            z[:, a, P * j:P * j + P], z[:, 2 + a, P * j:SEQ],
                                            start=True, stop=True)
                last.then_inc(inner_full, 1)

            def weighted_values(bank, weights, a):
                for j in range(TT):
                    last = nc.tensor.matmul(ps[:, bank, P * j:SEQ], z_v[:, j, a, :],
                                            weights[:, COL_AT[j]:COL_AT[j] + SEQ - P * j],
                                            start=j == 0, stop=j == TT - 1)
                return last

            def ret_out(p):
                pe.wait_ge(z_done, N_RET + 5 * p + 5)
                pe.wait_ge(inner_ready, 2 * p + 2)
                for a in range(2):
                    weighted_values(4 + a, sm[a], a).then_inc(ret_full, 1)

            def ret_var(p):
                pe.wait_ge(sq_ready, p + 1)
                for a in range(2):
                    last = nc.tensor.matmul(ps[:, 4 + a, :], ones[:, :], z[:, a, :], start=True, stop=True)
                last.then_inc(var_full, 1)

            def ret_turn(p, prev):
                g, v = N_RET + 5 * p, V_RET + 40 * p
                tail = {1: [lambda: ret_out(p - 1)], 3: [lambda: ret_var(p - 1)]} if prev else {1: [iw_turn_over]}
                pe.wait_ge(z_done, g if isinstance(p, int) and p == 0 else g - 2)
                at_least(pe, inner_ready, 2 * p)
                group(v, g, proj(6), tail, banks_free=False)
                if isinstance(p, int) and p == 0:
                    pe.wait_ge(z_done, g)
                group(v + 8, g + 1, proj(0), {4: [lambda: idx_scores(p, 0)], 6: [lambda: idx_scores(p, 1)]},
                      banks_free=True)
                at_least(pe, z_done, g)
                group(v + 16, g + 2, proj(2), {0: [lambda: idx_scores(p, 2)], 2: [lambda: idx_scores(p, 3)]},
                      banks_free=False)
                pe.wait_ge(z_done, g + 2)
                group(v + 24, g + 3, proj(0), {1: [lambda: inner(p, 0)], 4: [lambda: inner(p, 1)]})
                pe.wait_ge(z_done, g + 3)
                group(v + 32, g + 4, in_rows(2, h_hi, h_lo, TT, 2))

            ret_turn(0, False)
            with pe.Fori(1, NPAIR) as p:
                ret_turn(p, True)
            up_phase(V_UPR, N_UPR, 8, 12, {1: [lambda: ret_out(3)], 3: [lambda: ret_var(3)]})

            def dsa_logits(p, a):
                pe.wait_ge(z_done, N_DSA + 4 * p + 2)
                at_least(pe, logit_read, MEM_HEADS + 2 * p + a)
                at_least(pe, pt_ready, MEM_HEADS + 2 * p)
                at_least(pe, y_done, 12 + 2 * p)
                for b in range(TT):
                    w = P * (b + 1)
                    last = nc.tensor.matmul(flat[:, PACKED + ROW_AT[b]:PACKED + ROW_AT[b] + w],
                                            z[:, 2 + a, P * b:P * b + P], z[:, a, 0:w], start=True, stop=True)
                last.then_inc(logit_full, 1)

            def dsa_turn_over(p, a):
                pe.wait_ge(p_ready, MEM_HEADS + 2 * p + a + 1)
                pe.wait_ge(pt_ready, MEM_HEADS + 2 * p + a)
                for j in range(TT):
                    for b in range(j, TT):
                        at = PACKED + COL_AT[j] + P * (b - j)
                        last = nc.tensor.transpose(flat[:, at:at + P],
                                                   pr[a][:, ROW_AT[b] + P * j:ROW_AT[b] + P * j + P], ident[:, :])
                last.then_inc(pt_full, 1)

            def dsa_out(p, a):
                pe.wait_ge(z_done, N_DSA + 4 * p + 4)
                pe.wait_ge(pt_ready, MEM_HEADS + 2 * p + 2)
                weighted_values((7, 4)[a], pt[a], a).then_inc(o_full, 1)

            def dsa_turn(p, prev):
                g, v = N_DSA + 4 * p, V_DSA + 32 * p
                tail = {1: [lambda: dsa_out(p - 1, 0)], 3: [lambda: dsa_out(p - 1, 1)]} if prev else {}
                if not prev:
                    pe.wait_ge(sig_ready, 16)
                group(v, g, proj(0), tail)
                group(v + 8, g + 1, proj(2))
                group(v + 16, g + 2, proj(0), {1: [lambda: dsa_logits(p, 0)], 4: [lambda: dsa_logits(p, 1)]})
                group(v + 24, g + 3, in_rows(2, h_hi, h_lo, TT, 2),
                      {2: [lambda: dsa_turn_over(p, 0)], 5: [lambda: dsa_turn_over(p, 1)]})

            dsa_turn(0, False)
            with pe.Fori(1, NPAIR) as p:
                dsa_turn(p, True)
            up_phase(V_UPD, N_UPD, 16, 20, {1: [lambda: dsa_out(3, 0)], 3: [lambda: dsa_out(3, 1)]})

            pe.wait_ge(sig_ready, 24)
            pe.wait_ge(z_done, N_OUT)
            for g in range(4):
                at_least(pe, out_done, 4 * (g - 1))
                for k in range(16):
                    pe.wait_ge(lo_ready, V_OUT + 16 * g + k + 1)
                    if g == 0:
                        pe.wait_ge(m_lo_done, k + 1)
                    s = k % 4
                    wh = w_hi[:, s, :, :].rearrange("p a n -> p (a n)")
                    wl = w_lo[:, s, :, :].rearrange("p a n -> p (a n)")
                    for t in range(TT):
                        dst, tok = ps[:, 4 * (g % 2) + t, :], slice(P * t, P * t + P)
                        nc.tensor.matmul(dst, m_hi[:, k, tok], wh, start=k == 0, stop=False)
                        nc.tensor.matmul(dst, m_lo[:, k, tok], wh, start=False, stop=False)
                        last = nc.tensor.matmul(dst, m_hi[:, k, tok], wl, start=False, stop=k == 15)
                    last.then_inc(half_used, 1)

        @block.vector
        def _(dve):
            st = Steps(dve, own)
            V = nc.vector

            def rsqrt(a, y, u):
                st.then(V.tensor_scalar(u.bitcast(I32), a.bitcast(I32), 1, None, ALU.logical_shift_right))
                st.then(V.tensor_scalar(y.bitcast(I32), u.bitcast(I32), -1.0, RSQRT_SEED, ALU.mult, ALU.add))
                for _ in range(3):
                    st.then(V.scalar_tensor_tensor(out=u, in0=y, scalar=-0.5, in1=y, op0=ALU.mult, op1=ALU.mult))
                    st.then(V.tensor_tensor(u, u, a, ALU.mult))
                    st.then(V.scalar_tensor_tensor(out=y, in0=u, scalar=1.5, in1=y, op0=ALU.add, op1=ALU.mult))

            dve.wait_ge(norm_t, 1)
            V.tensor_copy(norm_w[:, 0:32], ps[:, 7, 0:32])
            V.tensor_scalar(norm_w[:, 32:40], ps[:, 7, 32:40], 0.25, None, ALU.mult).then_inc(norm_ready, 1)
            V.memset(stat[:, 1:3, :], 1.0)
            dve.wait_ge(consts, 11)
            V.tensor_scalar(negtri[:, :], iota_f[:, 0:P], 0.0, NEG, ALU.is_gt, ALU.mult)
            dve.wait_ge(sq_done, MT + TT)
            st.then(V.tensor_scalar(stat[:, 0, 0:6], stat[:, 0, 0:6], 1.0 / D, EPS, ALU.mult, ALU.add))
            rsqrt(stat[:, 0, 0:6], stat[:, 1, 0:6], stat[:, 2, 0:6])
            for t in range(MT):
                V.tensor_scalar(mem_rows[:, t, :], mem_rows[:, t, :], stat[:, 1, 4 + t:5 + t], None,
                                ALU.mult).then_inc(row_scaled, 1)
            for t in range(TT):
                V.tensor_scalar(x_rows[:, t, :], x_rows[:, t, :], stat[:, 1, t:t + 1], None,
                                ALU.mult).then_inc(row_scaled, 1)
            for n in range(2 * KT):
                k = n % KT
                dve.wait_ge(t_hi, n + 1)
                hi_t, lo_t, cols = (memt_hi, memt_lo, MEM) if n < KT else (h_hi, h_lo, SEQ)
                col = k + (KT if n < KT else 0)
                V.scalar_tensor_tensor(out=lo_t[:, k, :], in0=ps[:, n % 8, 0:cols], scalar=norm_w[:, col:col + 1],
                                       in1=hi_t[:, k, :].bitcast(F32), op0=ALU.mult,
                                       op1=ALU.subtract).then_inc(t_lo, 1)

            def take_km(i, e):
                dve.wait_ge(half_used, V_KV + 8 + 8 * e + 16 * i)
                V.tensor_copy(km[:, bass.ds(4 * i + 2 * e, 2), :],
                              ps[:, 2 * e:2 * e + 2, 0:MEM]).then_inc(z_done, 1)

            def take_vm(i, e):
                dve.wait_ge(half_used, V_KV + 8 + 8 * e + 16 * i)
                V.tensor_scalar(vm[:, :, bass.ds(GC * 2 * (i - 2) + GC * e, GC)], ps[:, 2 * e:2 * e + 2, 0:GC],
                                0.25, None, ALU.mult).then_inc(z_done, 1)
            for take, lo_i in ((take_km, 0), (take_vm, 2)):
                with dve.Fori(lo_i, lo_i + 2) as i:
                    take(i, 0)
                    take(i, 1)

            def silu_gate(bank, tanhs):
                dve.wait_ge(tanh_done, tanhs)
                ins = V.scalar_tensor_tensor(out=z[:, 4:6, :], in0=z[:, 4:6, :], scalar=1.0,
                                             in1=ps[:, bank:bank + 2, :], op0=ALU.add, op1=ALU.mult)
                ins.then_inc(z_done, 1)
                st.then(V.tensor_copy(top8[:, 0:1], logg[:, 0:1]))

            def mem_finish(h):
                silu_gate(2, h + 1)
                st.then(V.tensor_copy(v_mem[:, :, :], vm[:, :, bass.ds(MEM_HD * h, MEM_HD)]))
                dve.wait_ge(pt_full, h + 1)
                V.tensor_copy(pt_mem[:, :, :], ps[:, 6:8, :]).then_inc(pt_ready, 1)
                dve.wait_ge(o_full, h + 1)
                write_y(2 * h, ps[:, 4:6, :], z[:, 4:6, :], z[:, 0:2, :], 1)

            def write_y(tile, a, b, tmp, signals):
                w = tmp.shape[1]
                dst_hi, dst_lo = y_hi[:, bass.ds(tile, w), :], y_lo[:, bass.ds(tile, w), :]
                st.then(V.tensor_tensor(tmp, a, b, ALU.mult))
                st.then(V.tensor_copy(dst_hi, tmp))
                V.tensor_tensor(dst_lo, tmp, dst_hi.bitcast(F32), ALU.subtract).then_inc(y_done, signals)

            def mem_turn(h, prev):
                if prev:
                    mem_finish(h - 1)
                dve.wait_ge(half_used, V_MEM + 8 + 16 * h)
                V.tensor_scalar(z[:, 2:4, :], ps[:, 0:2, :], MEM_HD ** -0.5, None, ALU.mult).then_inc(z_done, 1)
                dve.wait_ge(logit_full, h + 1)
                st.then(V.tensor_copy(p_mem[:, :, :].rearrange("p t m -> p (t m)"), flat[:, 2048:3072]))
                V.tensor_reduce(rmax[:, 0, :], p_mem[:, :, :], AX.X, ALU.max, negate=True).then_inc(neg_max, 1)
                V.tensor_copy(top8[:, 0:1], logg[:, 0:1]).then_inc(logit_read, 1)
                dve.wait_ge(exp_done, h + 1)
                st.then(V.reciprocal(rinv[:, 0, :], rsum[:, 0, :]))
                for b in range(TT):
                    ins = V.tensor_scalar(p_mem[:, b, :], p_mem[:, b, :], rinv[:, 0, b:b + 1], None, ALU.mult)
                ins.then_inc(p_ready, 1)

            mem_turn(0, False)
            with dve.Fori(1, MEM_HEADS) as h:
                st.enter(h, 1, 6)
                mem_turn(h, True)
                st.leave(MEM_HEADS - 1, 6)

            def up_phase(v0, g0, sig0, first_branch, finish, extra=None, per=0):
                def turn(i, first):
                    for e in range(2):
                        g = g0 + 4 * i + 2 * e
                        if first and e == 0:
                            finish()
                        dve.wait_ge(half_used, v0 + 12 + 12 * e + 24 * i)
                        dve.wait_ge(sig_ready, sig0 + 2 * i + e + 1)
                        tiles = merged[:, bass.ds(4 * i + 2 * e, 2), :]
                        if first_branch:
                            V.scalar_tensor_tensor(out=tiles, in0=z[:, 0:2, :], scalar=1.0, in1=ps[:, 2:4, :],
                                                   op0=ALU.add, op1=ALU.mult).then_inc(z_done, 2)
                        else:
                            st.then(V.scalar_tensor_tensor(out=z[:, 2:4, :], in0=z[:, 0:2, :], scalar=1.0,
                                                           in1=ps[:, 2:4, :], op0=ALU.add, op1=ALU.mult))
                            V.tensor_tensor(tiles, tiles, z[:, 2:4, :], ALU.add).then_inc(z_done, 2)
                        if extra:
                            extra(i, e)
                turn(0, True)
                if extra:
                    for i in range(1, 4):
                        turn(i, False)
                    return
                with dve.Fori(1, 4) as i:
                    st.enter(i, 1, per)
                    turn(i, False)
                    st.leave(3, per)

            up_phase(V_UPM, N_UPM, 0, True, lambda: mem_finish(3))

            dve.wait_ge(half_used, V_IKW + 8)
            V.tensor_copy(ikt[0:IDX_DIM, :], ps[0:IDX_DIM, 6, :])
            V.tensor_copy(ikt[IDX_DIM:2 * IDX_DIM, :], ps[0:IDX_DIM, 6, :])
            V.tensor_scalar(iwt[:, :], ps[IDX_DIM:IKW, 6, :], (IDX_HEADS ** -0.5) * (IDX_DIM ** -0.5), None,
                            ALU.mult).then_inc(iwt_ready, 1)
            V.memset(score[:, :, :], 0.0).then_inc(z_done, 1)
            dve.wait_ge(iwt_full, 1)
            V.tensor_copy(iw[:, :, :].rearrange("p t h -> p (t h)"),
                          ps[:, 4, 0:TT * IDX_HEADS]).then_inc(iw_ready, 1)

            def ret_finish(p):
                o, a, y, u = z[:, 2:4, :], z[:, 0:2, :], z[:, 6:8, :], iq[:, :, :]
                dve.wait_ge(ret_full, 2 * p + 2)
                st.then(V.tensor_copy(o, ps[:, 4:6, :]))
                V.tensor_tensor(a, o, o, ALU.mult).then_inc(sq_ready, 1)
                dve.wait_ge(var_full, p + 1)
                V.tensor_scalar(a, ps[:, 4:6, :], GN_EPS, None, ALU.add).then_inc(var_read, 1)
                st.then(V.tensor_copy(top8[:, 0:1], logg[:, 0:1]))
                rsqrt(a, y, u)
                for b in range(2):
                    ins = V.scalar_tensor_tensor(out=o[:, b, :], in0=o[:, b, :],
                                                 scalar=norm_w[:, bass.ds(2 * KT + 2 * p + b, 1)],
                                                 in1=y[:, b, :], op0=ALU.mult, op1=ALU.mult)
                st.then(ins)
                write_y(2 * p, o, z[:, 4:6, :], a, 2)

            def ret_turn(p, prev):
                g = N_RET + 5 * p
                if prev:
                    ret_finish(p - 1)
                dve.wait_ge(half_used, V_RET + 8 + 40 * p)
                V.tensor_copy(iq[:, :, :], ps[:, 6:8, :]).then_inc(z_done, 1)
                dve.wait_ge(half_used, V_RET + 16 + 40 * p)
                V.tensor_scalar(z[:, 0:2, :], ps[:, 0:2, :], HD ** -0.5, None, ALU.mult).then_inc(z_done, 1)
                for n in range(4):
                    dve.wait_ge(relu_done, 4 * p + n + 1)
                    for b in range(TT):
                        w = P * (b + 1)
                        ins = V.scalar_tensor_tensor(out=score[:, b, 0:w], in0=sm[n % 2][:, ROW_AT[b]:ROW_AT[b] + w],
                                                     scalar=iw[:, b, bass.ds(4 * p + n, 1)], in1=score[:, b, 0:w],
                                                     op0=ALU.mult, op1=ALU.add)
                    ins.then_inc(relu_used, 1)
                    if n == 3:
                        dve.wait_ge(half_used, V_RET + 24 + 40 * p)
                        V.tensor_copy(z[:, 2:4, :], ps[:, 2:4, :]).then_inc(z_done, 1)
                    dve.wait_ge(relu_used, 4 * p + n + 1)
                for a in range(2):
                    dve.wait_ge(decay_ready, 2 * p + a + 1)
                    st.then(V.scalar_tensor_tensor(out=decay[:, 0:P], in0=iota_f[:, 0:P], scalar=0.0,
                                                   in1=decay[:, 0:P], op0=ALU.is_ge, op1=ALU.mult))
                    dve.wait_ge(inner_full, 2 * p + a + 1)
                    for j in range(TT):
                        w = SEQ - P * j
                        at = COL_AT[j]
                        ins = V.tensor_tensor(sm[a][:, at:at + w], flat[:, PACKED + at:PACKED + at + w],
                                              decay[:, 0:w], ALU.mult)
                    ins.then_inc(inner_ready, 1)
                silu_gate(0, MEM_HEADS + p + 1)
                dve.wait_ge(half_used, V_RET + 40 + 40 * p)
                rows = flat[:, 1024:2048].rearrange("p (t h d) -> p (t h) d", h=2, d=HD)
                st.then(V.tensor_reduce(stat[:, 0, :], rows, AX.X, ALU.add))
                st.then(V.tensor_scalar(stat[:, 0, :], stat[:, 0, :], 1.0 / HD, None, ALU.mult))
                V.tensor_tensor(z_v.rearrange("p t h d -> p (t h) d"), rows,
                                stat[:, 0, :].unsqueeze(2).to_broadcast([P, 8, HD]),
                                ALU.subtract).then_inc(z_done, 1)

            RET_STEPS = 21
            ret_turn(0, False)
            with dve.Fori(1, NPAIR) as p:
                st.enter(p, 1, RET_STEPS)
                ret_turn(p, True)
                st.leave(NPAIR - 1, RET_STEPS)

            def select_keys(i, e):
                row, dst = score[:, i, :], far[:, i, :]
                if e == 0:
                    st.then(V.tensor_copy(top8[:, 0:1], logg[:, 0:1]))
                for _ in range(TOPK // 16):
                    st.then(V.max(out=top8[:, :], in_=row))
                    st.then(V.match_replace(out=row, in_to_replace=top8[:, :], in_values=row, imm_value=TAKEN))
                if e == 1:
                    st.then(V.tensor_scalar(row, row, TAKEN / 2, FAR, ALU.is_gt, ALU.mult))
                    st.then(V.tensor_tensor(row, row, iota_f[:, :], ALU.subtract))
                    V.tensor_scalar(dst, row, float(P * i), None, ALU.add)
                    st.then(V.tensor_copy(top8[:, 0:1], logg[:, 0:1]))

            def ret_end():
                ret_finish(3)
                for b in range(TT):
                    if b < TT - 1:
                        V.memset(score[:, b, P * (b + 1):SEQ], NEG)
                    V.tensor_tensor(score[:, b, P * b:P * b + P], score[:, b, P * b:P * b + P], negtri[:, :], ALU.add)

            up_phase(V_UPR, N_UPR, 8, False, ret_end, select_keys)
            for b in range(TT):
                d = far[:, b, P * b:P * b + P]
                st.then(V.scalar_tensor_tensor(out=d, in0=negtri[:, :], scalar=-FAR / 1e30, in1=d,
                                               op0=ALU.mult, op1=ALU.add) if False else
                        V.scalar_tensor_tensor(out=d, in0=negtri[:, :], scalar=FAR / NEG, in1=d,
                                               op0=ALU.mult, op1=ALU.add))

            def dsa_finish(p):
                for a in range(2):
                    dve.wait_ge(o_full, MEM_HEADS + 2 * p + a + 1)
                    write_y(2 * p + a, ps[:, (7, 4)[a]:(7, 4)[a] + 1, :], z[:, 4 + a:5 + a, :], z[:, 3:4, :], 1)
                    st.then(V.tensor_copy(top8[:, 0:1], logg[:, 0:1]))

            def dsa_turn(p, prev):
                g = N_DSA + 4 * p
                if prev:
                    dsa_finish(p - 1)
                dve.wait_ge(half_used, V_DSA + 8 + 32 * p)
                V.tensor_scalar(z[:, 0:2, :], ps[:, 0:2, :], HD ** -0.5, None, ALU.mult).then_inc(z_done, 1)
                dve.wait_ge(half_used, V_DSA + 16 + 32 * p)
                V.tensor_copy(z[:, 2:4, :], ps[:, 2:4, :]).then_inc(z_done, 1)
                for a in range(2):
                    dve.wait_ge(logit_full, MEM_HEADS + 2 * p + a + 1)
                    for b in range(TT):
                        w, at = P * (b + 1), ROW_AT[b]
                        ins = V.scalar_tensor_tensor(out=pr[a][:, at:at + w], in0=far[:, b, 0:w],
                                                     scalar=slope[:, bass.ds(2 * p + a, 1)],
                                                     in1=flat[:, PACKED + at:PACKED + at + w],
                                                     op0=ALU.mult, op1=ALU.add)
                    ins.then_inc(logit_read, 1)
                    dve.wait_ge(logit_read, MEM_HEADS + 2 * p + a + 1)
                    for b in range(TT):
                        w, at = P * (b + 1), ROW_AT[b]
                        ins = V.tensor_reduce(rmax[:, a, b:b + 1], pr[a][:, at:at + w], AX.X, ALU.max, negate=True)
                    ins.then_inc(neg_max, 1)
                for a in range(2):
                    dve.wait_ge(exp_done, MEM_HEADS + 2 * p + a + 1)
                    st.then(V.reciprocal(rinv[:, a, :], rsum[:, a, :]))
                    for b in range(TT):
                        w, at = P * (b + 1), ROW_AT[b]
                        ins = V.tensor_scalar(pr[a][:, at:at + w], pr[a][:, at:at + w], rinv[:, a, b:b + 1], None,
                                              ALU.mult)
                    ins.then_inc(p_ready, 1)
                for a in range(2):
                    dve.wait_ge(pt_full, MEM_HEADS + 2 * p + a + 1)
                    V.tensor_copy(pt[a][:, :], flat[:, PACKED:PACKED + PACK]).then_inc(pt_ready, 1)
                    if a == 0:
                        silu_gate(0, MEM_HEADS + NPAIR + p + 1)
                dve.wait_ge(half_used, V_DSA + 32 + 32 * p)
                V.tensor_scalar(z_v.rearrange("p t h d -> p (t h d)"), flat[:, 1024:2048], 0.25, None,
                                ALU.mult).then_inc(z_done, 1)

            DSA_STEPS = 9
            dsa_turn(0, False)
            with dve.Fori(1, NPAIR) as p:
                st.enter(p, 1, DSA_STEPS)
                dsa_turn(p, True)
                st.leave(NPAIR - 1, DSA_STEPS)
            up_phase(V_UPD, N_UPD, 16, False, lambda: dsa_finish(3), None, 2)

            for k in range(KT):
                dve.wait_ge(m_hi_done, k + 1)
                V.tensor_tensor(m_lo[:, k, :], merged[:, k, :], m_hi[:, k, :].bitcast(F32),
                                ALU.subtract).then_inc(m_lo_done, 1)
            dve.wait_ge(post_in, 16)
            for g in range(4):
                for t in range(TT):
                    dve.wait_ge(out_sq, 4 * g + t + 1)
                    V.tensor_tensor(o_rows[:, t, 512 * g:512 * g + 512], ps[:, 4 * (g % 2) + t, :],
                                    post_w[:, 512 * g:512 * g + 512], ALU.mult).then_inc(out_done, 1)
            st.then(V.tensor_reduce(stat[:, 0, 0:TT], ssq[:, :, :], AX.X, ALU.add))
            st.then(V.tensor_scalar(stat[:, 0, 0:TT], stat[:, 0, 0:TT], 1.0 / D, EPS, ALU.mult, ALU.add))
            rsqrt(stat[:, 0, 0:TT], stat[:, 1, 0:TT], stat[:, 2, 0:TT])
            dve.wait_ge(again_in, 16)
            for t in range(TT):
                V.scalar_tensor_tensor(out=o_rows[:, t, :], in0=o_rows[:, t, :], scalar=stat[:, 1, t:t + 1],
                                       in1=x_again[:, t, :], op0=ALU.mult, op1=ALU.add).then_inc(final, 1)


_INS = ["x", "mem", "pre_norm_w", "w_in", "ret_gn_w", "mem_norm_w", "w_mem_kv", "w_up_ret", "w_up_dsa",
        "w_up_mem", "w_o", "post_norm_w"]


def kernel(**inputs):
    import numpy as _np
    import concourse.bacc as _bacc
    from concourse import mybir as _mybir
    from concourse.bass_utils import run_bass_kernel_spmd as _run

    nc = _bacc.Bacc("TRN2", target_bir_lowering=False, num_devices=1)
    arrays, args = {}, []
    for name in _INS:
        a = _np.ascontiguousarray(inputs[name])
        arrays[f"in_{name}"] = a
        args.append(nc.dram_tensor(f"in_{name}", a.shape, _mybir.dt.from_np(a.dtype), kind="ExternalInput").ap())
    args.append(nc.dram_tensor("out_0", (1, SEQ, D), F32, kind="ExternalOutput").ap())
    build(nc, *args)
    r = _run(nc, [arrays], core_ids=[0])
    return r.results[0]["out_0"]
```

```python
from contextlib import ExitStack

import numpy as np

import concourse.bass as bass
from concourse import mybir

F32 = mybir.dt.float32
F32R = mybir.dt.float32r
I32 = mybir.dt.int32
ALU = mybir.AluOpType
ACT = mybir.ActivationFunctionType
AX = mybir.AxisListType

P = 128
SEQ = 512
D = 2048
KT = D // P
TT = SEQ // P
MEM = 256
MT = MEM // P
HD = 128
WIDTH = 1024
NPAIR = WIDTH // 256
IDX_HEADS = 16
IDX_DIM = 64
TOPK = min(256, SEQ // 4)
MEM_HEADS = 4
MEM_HD = 256
GC = 256
EPS = 1e-6
GN_EPS = 1e-5
NEG = -1e30
TAKEN = -3e38
FAR = 1e32
RSQRT_SEED = float(0x5F3759DF)

RQ, RK, RV, RG, AQ, AK, AV, AG, IQ, IK = [WIDTH * n for n in range(10)]
IKW = IDX_DIM + IDX_HEADS
MQ = IK + IKW
MG = MQ + WIDTH
G_RET = MG + WIDTH
G_DSA = G_RET + D
G_MEM = G_DSA + D

ROW_AT = {0: 896, 1: 1024, 2: 512, 3: 0}
COL_AT = {0: 0, 1: 512, 2: 1024, 3: 896}
PACK = 1280

V_KV, V_MEM = 0, 64
V_UPM = V_MEM + 4 * 16
V_IKW = V_UPM + 8 * 12
V_RET = V_IKW + 8
V_UPR = V_RET + 4 * 40
V_DSA = V_UPR + 8 * 12
V_UPD = V_DSA + 4 * 32
V_OUT = V_UPD + 8 * 12
V_END = V_OUT + 4 * 16
N_KV, N_MEM, N_UPM, N_IKW, N_RET = 0, 8, 16, 32, 33
N_UPR = N_RET + 20
N_DSA = N_UPR + 16
N_UPD = N_DSA + 16
N_OUT = N_UPD + 16


def at_least(eng, sem, value):
    if isinstance(value, int) and value <= 0:
        return
    eng.wait_ge(sem, value)


class Steps:

    def __init__(self, eng, sem):
        self.eng, self.sem, self.base, self.n = eng, sem, 0, 0

    def then(self, ins):
        self.n += 1
        ins.then_inc(self.sem, 1)
        self.eng.wait_ge(self.sem, self.base + self.n)

    def enter(self, i, first, per):
        self.start = self.base + self.n
        self.base, self.n = self.start + (i - first) * per, 0

    def leave(self, turns, per):
        assert self.n == per, (self.n, per)
        self.base, self.n = self.start + turns * per, 0


def build(nc, x, mem, pre_norm_w, w_in, ret_gn_w, mem_norm_w, w_mem_kv, w_up_ret, w_up_dsa,
          w_up_mem, w_o, post_norm_w, out):
    with ExitStack() as ctx:
        base = 16640
        used = [base]

        def place(name, shape, dt=F32, at=None):
            size = 4 * int(np.prod(shape[1:]))
            if at is None:
                at = used[0]
                used[0] += (size + 31) // 32 * 32
            return nc.alloc_sbuf_tensor_at(name, shape, dt, offset=at), at

        def sem(name):
            return ctx.enter_context(nc.semaphore(name))

        h_hi, at_h = place("h_hi", [P, KT, SEQ], F32R)
        h_lo, at_hl = place("h_lo", [P, KT, SEQ], F32R)
        raw, _ = place("raw", [P, 4, 4, GC])
        w_hi, _ = place("w_hi", [P, 4, 2, GC], F32R)
        w_lo, _ = place("w_lo", [P, 4, 2, GC], F32R)
        y_hi, at_y = place("y_hi", [P, 8, SEQ], F32R)
        y_lo, _ = place("y_lo", [P, 8, SEQ], F32R)
        merged, at_m = place("merged", [P, KT, SEQ])
        z, at_z = place("z", [P, 8, SEQ])
        z_v = z[:, 6:8, :].rearrange("p a (t d) -> p (a t) d", t=4).rearrange(
            "p (t h) d -> p t h d", h=2)
        far, at_far = place("far", [P, 2048])
        iota_f, _ = place("iota_f", [P, SEQ])
        negtri, _ = place("negtri", [P, P])
        ident, _ = place("ident", [P, P])
        ones, _ = place("ones", [P, P])
        logg, _ = place("logg", [P, 8])
        slope, _ = place("slope", [P, 8])
        norm_w, _ = place("norm_w", [P, 40])
        stat, _ = place("stat", [P, 3, 8])
        top8, _ = place("top8", [P, 8])
        rmax, _ = place("rmax", [P, 2, 4])
        rsum, _ = place("rsum", [P, 2, 4])
        rinv, _ = place("rinv", [P, 2, 4])
        ssq, _ = place("ssq", [P, TT, 4])
        at_x = used[0]

        x_rows, _ = place("x_rows", [P, TT, D], at=at_m)
        mem_rows, _ = place("mem_rows", [P, MT, D], at=at_z)
        memt_hi, _ = place("memt_hi", [P, KT, MEM], F32R, at=at_y)
        memt_lo, _ = place("memt_lo", [P, KT, MEM], F32R, at=at_y + 16384)
        junk, _ = place("junk", [P, D], at=at_x + 8192)
        junk_act, _ = place("junk_act", [P, D], at=at_far)
        norm_rows, _ = place("norm_rows", [40, P], at=at_x)
        iota_i, _ = place("iota_i", [P, SEQ], I32, at=at_x + 512)
        km, _ = place("km", [P, 8, MEM], at=at_far)
        vm, _ = place("vm", [P, MT, WIDTH], at=at_x)
        p_mem, _ = place("p_mem", [P, TT, MEM], at=at_x + 8192)
        pt_mem, _ = place("pt_mem", [P, MT, SEQ], at=at_x + 12288)
        v_mem, _ = place("v_mem", [P, MT, MEM_HD], at=at_x + 16384)
        sm_a, _ = place("sm_a", [P, PACK], at=at_far)
        ik_hi, _ = place("ik_hi", [P, SEQ], F32R, at=at_far + 5120)
        iw, _ = place("iw", [P, TT, IDX_HEADS], at=at_far + 7168)
        score, _ = place("score", [P, PACK], at=at_x)
        sm_b, _ = place("sm_b", [P, PACK], at=at_x + 5120)
        iq = [place("iq_a", [P, 2, SEQ], F32R, at=at_x + 10240)[0],
              place("iq_b", [P, 2, SEQ], F32R, at=at_z + 8192)[0]]
        scratch, _ = place("scratch", [P, 2, SEQ], at=at_x + 10240)
        decay, _ = place("decay", [P, SEQ], at=at_x + 14336)
        iwt, _ = place("iwt", [IDX_HEADS, SEQ], at=at_x + 14336)
        ik_lo, _ = place("ik_lo", [P, SEQ], F32R, at=at_x + 16384)
        assert at_x + 18432 <= nc.sbuf_usable_end, (at_x, nc.sbuf_usable_end)
        pr = [place("p_a", [P, PACK], at=at_x)[0], place("p_b", [P, PACK], at=at_x + 5120)[0]]
        pt = [place("pt_a", [P, PACK], at=at_x + 10240)[0], place("pt_b", [P, PACK], at=at_z)[0]]
        m_hi, _ = place("m_hi", [P, KT, SEQ], F32R, at=at_h)
        m_lo, _ = place("m_lo", [P, KT, SEQ], F32R, at=at_hl)
        o_rows, _ = place("o_rows", [P, TT, D], at=at_y)
        x_again, _ = place("x_again", [P, TT, D], at=at_m)
        post_w, _ = place("post_w", [P, D], at=at_far)
        sq_out, _ = place("sq_out", [P, 1024], at=at_x)
        sm = [sm_a, sm_b]

        ps = ctx.enter_context(nc.psum_tensor("ps", [P, 8, 512], F32))
        flat = ps[:, :, :].rearrange("p b n -> p (b n)")
        PACKED = 4 * 512

        raw_in = [sem(f"raw_in{i}") for i in range(4)]
        hi_ready, lo_ready, half_used = sem("hi_ready"), sem("lo_ready"), sem("half_used")
        z_done, sig_ready = sem("z_done"), sem("sig_ready")
        small_in = sem("small_in")
        mem_in, x_in = [sem(f"mem_in{t}") for t in range(MT)], [sem(f"x_in{t}") for t in range(TT)]
        consts, pool_own = sem("consts"), sem("pool_own")
        sq_done, sq_rows, row_scaled, t_ready, t_hi, t_lo = (sem("sq_done"), sem("sq_rows"), sem("row_scaled"), sem("t_ready"),
                                                    sem("t_hi"), sem("t_lo"))
        norm_t, norm_ready = sem("norm_t"), sem("norm_ready")
        logit_full, logit_read, neg_max, exp_done, p_ready = (
            sem("logit_full"), sem("logit_read"), sem("neg_max"), sem("exp_done"), sem("p_ready"))
        pt_full, pt_ready, o_full, y_done, tanh_done = (
            sem("pt_full"), sem("pt_ready"), sem("o_full"), sem("y_done"), sem("tanh_done"))
        iwt_ready, iwt_full, iw_ready = sem("iwt_ready"), sem("iwt_full"), sem("iw_ready")
        idx_full, relu_done, relu_used = sem("idx_full"), sem("relu_done"), sem("relu_used")
        decay_ready, inner_full, inner_ready = sem("decay_ready"), sem("inner_full"), sem("inner_ready")
        ret_full, sq_ready, var_full, var_read = (sem("ret_full"), sem("sq_ready"), sem("var_full"),
                                                  sem("var_read"))
        m_hi_done, m_lo_done = sem("m_hi_done"), sem("m_lo_done")
        out_sq, out_done = sem("out_sq"), sem("out_done")
        again_in, post_in, final, stored, own = (sem("again_in"), sem("post_in"), sem("final"), sem("stored"),
                                                 sem("own"))

        def by_units(w):
            return w.rearrange("(u t p) n -> u p t n", t=4, p=P)

        win_u, wkv_u = by_units(w_in[0]), by_units(w_mem_kv[0])
        up_u = {"m": by_units(w_up_mem[0]), "r": by_units(w_up_ret[0]), "d": by_units(w_up_dsa[0])}
        wo_u = w_o[0].rearrange("(u t p) n -> u p t n", t=2, p=P)
        x_t = x[0].rearrange("(t p) d -> t p d", p=P)
        mem_t = mem[0].rearrange("(t p) d -> p t d", p=P)
        out_t = out[0].rearrange("(t p) d -> t p d", p=P)

        block = ctx.enter_context(nc.Block())

        @block.sync
        def _(sp):
            def unit(v, slot, src, cols=GC):
                at_least(sp, lo_ready, v - 6)
                sp.dma_start(raw[:, slot, :, 0:cols], src).then_inc(raw_in[slot], 16)

            def group(v, col, view=win_u, slot0=0, cols=GC):
                for u in range(4):
                    unit(v + 2 * u, (slot0 + u) % 4, view[u, :, :, bass.ds(col, cols)], cols)

            def two_units(v, col, view, slot0):
                at_least(sp, lo_ready, v + 2 - 6)
                for u in (1, 0):
                    sp.dma_start(raw[:, slot0 + u, :, :],
                                 view[u, :, :, bass.ds(col, GC)]).then_inc(raw_in[slot0 + u], 16)

            sp.dma_start(norm_rows[0:16, :], pre_norm_w[0].rearrange("(k p) -> k p", p=P)).then_inc(small_in, 16)
            sp.dma_start(norm_rows[16:32, :], mem_norm_w[0].rearrange("(k p) -> k p", p=P)).then_inc(small_in, 16)
            sp.dma_start(norm_rows[32:40, :], ret_gn_w[0].rearrange("(k p) -> k p", p=P)).then_inc(small_in, 16)
            for t in range(MT):
                sp.dma_start(mem_rows[:, t, :], mem_t[:, t, :]).then_inc(mem_in[t], 16)
            group(V_KV, 0, wkv_u)
            for t in range(TT):
                sp.dma_start(x_rows[:, t, :], x_t[t]).then_inc(x_in[t], 16)
            with sp.Fori(1, 8) as g:
                group(V_KV + 8 * g, g * GC, wkv_u)
            with sp.Fori(0, MEM_HEADS) as h:
                group(V_MEM + 16 * h, MQ + GC * h)
                group(V_MEM + 8 + 16 * h, MG + GC * h)

            def up_phase(v0, gate_col, view):
                with sp.Fori(0, 4) as i:
                    for e in range(2):
                        v = v0 + 24 * i + 12 * e
                        group(v, gate_col + 2 * GC * i + GC * e, slot0=2 * e)
                        two_units(v + 8, 2 * GC * i + GC * e, view, 2 * e)

            up_phase(V_UPM, G_MEM, up_u["m"])
            group(V_IKW, IK, cols=IKW)
            with sp.Fori(0, NPAIR) as p:
                for n, part in enumerate((IQ, RK, RQ, RG, RV)):
                    v = V_RET + 8 * n + 40 * p
                    if part:
                        group(v, part + GC * p)
                    else:
                        two_units(v, part + GC * p, win_u, 0)
                        for u in (2, 3):
                            unit(v + 2 * u, u, win_u[u, :, :, bass.ds(part + GC * p, GC)])
            up_phase(V_UPR, G_RET, up_u["r"])
            with sp.Fori(0, NPAIR) as p:
                for n, part in enumerate((AK, AQ, AG, AV)):
                    group(V_DSA + 8 * n + 32 * p, part + GC * p)
            up_phase(V_UPD, G_DSA, up_u["d"])
            def out_group(g):
                for u in (1, 0, 2, 3, 4, 5, 6, 7):
                    if u > 0:
                        at_least(sp, lo_ready, V_OUT + 2 * u - 6 + 16 * g)
                    sp.dma_start(raw[:, u % 4, :, :].rearrange("p (t a) n -> p t (a n)", t=2),
                                 wo_u[u, :, :, bass.ds(512 * g, 512)]).then_inc(raw_in[u % 4], 16)
            out_group(0)
            sp.wait_ge(m_lo_done, KT)
            sp.dma_start(post_w[:, :], post_norm_w[0:1, :].broadcast_to([P, D])).then_inc(post_in, 16)
            sp.dma_start(x_again[:, :, :], x[0].rearrange("(t p) d -> p t d", p=P)).then_inc(again_in, 16)
            with sp.Fori(1, 4) as g:
                out_group(g)
            for t in range(TT):
                sp.wait_ge(final, t + 1)
                sp.dma_start(out_t[t], o_rows[:, t, :]).then_inc(stored, 16)
            sp.wait_ge(stored, 16 * TT)

        @block.gpsimd
        def _(pool):
            nc.gpsimd.memset(ident[:, :], 0.0).then_inc(pool_own, 1)
            nc.gpsimd.memset(ones[:, :], 1.0 / HD).then_inc(consts, 1)
            nc.gpsimd.iota(iota_i[:, :], pattern=[[1, SEQ]], base=0, channel_multiplier=-1).then_inc(pool_own, 1)
            pool.wait_ge(pool_own, 2)
            nc.gpsimd.affine_select(out=ident[:, :], in_=ident[:, :], compare_op=ALU.not_equal, fill=1.0,
                                    base=0, pattern=[[-1, P]], channel_multiplier=1).then_inc(consts, 1)
            nc.gpsimd.tensor_copy(iota_f[:, :], iota_i[:, :]).then_inc(consts, 1)
            for h in range(8):
                nc.gpsimd.memset(logg[:, h:h + 1], float(np.log1p(-(2.0 ** (-5.0 - h)))))
                nc.gpsimd.memset(slope[:, h:h + 1], -(2.0 ** (-(h + 1.0)))).then_inc(consts, 1)

            def lo(v, j, cols=GC):
                pool.wait_ge(hi_ready, v + 1)
                s = j % 4
                nc.gpsimd.tensor_tensor(w_lo[:, s, :, 0:cols],
                                        raw[:, (j // 2) % 4, 2 * (j % 2):2 * (j % 2) + 2, 0:cols],
                                        w_hi[:, s, :, 0:cols].bitcast(F32), ALU.subtract).then_inc(lo_ready, 1)

            with pool.Fori(0, (V_IKW - V_KV) // 8) as i:
                for j in range(8):
                    lo(V_KV + 8 * i + j, j)
            for j in range(8):
                lo(V_IKW + j, j, IKW)
            with pool.Fori(0, (V_END - V_RET) // 8) as i:
                for j in range(8):
                    lo(V_RET + 8 * i + j, j)

        @block.scalar
        def _(act):
            def hi(v, j, turn, cols=GC):
                slot = (j // 2) % 4
                act.wait_ge(raw_in[slot], 16 * turn + 16)
                at_least(act, half_used, v - 3)
                nc.scalar.activation(w_hi[:, j % 4, :, 0:cols],
                                     raw[:, slot, 2 * (j % 2):2 * (j % 2) + 2, 0:cols],
                                     ACT.Copy).then_inc(hi_ready, 1)

            def run(first, i, per, count, hooks):
                if isinstance(i, int):
                    v, turn = first + i * per, (first + i * per) // 8
                else:
                    v, turn = first + i * per, first // 8 + i * (per // 8)
                for k in range(count):
                    hi(v + k, k % 8, turn + k // 8)
                    for f in hooks.get(k, ()):
                        f()

            act.wait_ge(mem_in[0], 16)
            nc.scalar.activation(junk_act[:, :], mem_rows[:, 0, :], ACT.Square,
                                 accum_out=stat[:, 0, 4:5]).then_inc(sq_done, 1)

            def rows_hi(n):
                act.wait_ge(t_ready, n + 1)
                k = n % KT
                dst, bank, cols, col = ((memt_hi, k % 8, MEM, KT + k) if n < KT else
                                        (h_hi, 4 + k % 4, SEQ, k))
                nc.scalar.activation(dst[:, k, :], ps[:, bank, 0:cols], ACT.Copy,
                                     scale=norm_w[:, col:col + 1]).then_inc(t_hi, 1)
            act.wait_ge(norm_ready, 1)
            for n in range(KT):
                rows_hi(n)
            run(V_KV, 0, 32, 32, {16 + k: [lambda k=k: rows_hi(KT + k)] for k in range(KT)})
            with act.Fori(4, 8) as g:
                run(V_KV, g, 8, 8, {})

            def tanh_gate(bank, v):
                act.wait_ge(half_used, v)
                nc.scalar.activation(z[:, 4:6, :], ps[:, bank:bank + 2, :], ACT.Tanh,
                                     scale=0.5).then_inc(tanh_done, 1)

            def mem_turn(h, prev):
                def exps():
                    act.wait_ge(logit_read, h + 1)
                    softmax_exp_mem(h)
                hooks = {14: [exps]}
                if prev:
                    hooks[3] = [lambda: mem_tanh(h - 1)]
                run(V_MEM, h, 16, 16, hooks)

            def softmax_exp_mem(h):
                act.wait_ge(neg_max, h + 1)
                for b in range(TT):
                    ins = nc.scalar.activation(p_mem[:, b, :], p_mem[:, b, :], ACT.Exp,
                                               bias=rmax[:, 0, b:b + 1], accum_out=rsum[:, 0, b:b + 1])
                ins.then_inc(exp_done, 1)

            def mem_tanh(h):
                at_least(act, y_done, h)
                tanh_gate(2, V_MEM + 16 + 16 * h)

            mem_turn(0, False)
            with act.Fori(1, MEM_HEADS) as h:
                mem_turn(h, True)

            def up_phase(v0, g0, sig0, y_before, last_tanh):
                def turn(i, first):
                    def sig(e):
                        g = g0 + 4 * i + 2 * e
                        act.wait_ge(half_used, v0 + 8 + 12 * e + 24 * i)
                        act.wait_ge(z_done, g)
                        if first and e == 0:
                            act.wait_ge(y_done, y_before)
                        nc.scalar.activation(z[:, 0:2, :], ps[:, 0:2, :], ACT.Tanh,
                                             scale=0.5).then_inc(sig_ready, 1)
                    hooks = {11: [lambda: sig(0)], 23: [lambda: sig(1)]}
                    if first and last_tanh:
                        hooks[3] = [last_tanh]
                    run(v0, i, 24, 24, hooks)
                turn(0, True)
                with act.Fori(1, 4) as i:
                    turn(i, False)

            up_phase(V_UPM, N_UPM, 0, 4, lambda: mem_tanh(3))

            for j in range(8):
                hi(V_IKW + j, j, V_IKW // 8, IKW)

            def ret_turn(p):
                g0 = N_RET + 5 * p

                def relu(n):
                    act.wait_ge(idx_full, 4 * p + n + 1)
                    at_least(act, relu_used, 4 * p + n - 1)
                    if n < 2:
                        at_least(act, ret_full, 2 * p)
                    nc.scalar.activation(sm[n % 2][:, :], flat[:, PACKED:PACKED + PACK],
                                         ACT.Relu).then_inc(relu_done, 1)

                def decay_of(a):
                    at_least(act, inner_ready, 2 * p + a)
                    nc.scalar.activation(decay[:, :], iota_f[:, :], ACT.Exp,
                                         scale=logg[:, bass.ds(2 * p + a, 1)]).then_inc(decay_ready, 1)

                def tanh():
                    at_least(act, y_done, 4 + 2 * p)
                    tanh_gate(0, V_RET + 32 + 40 * p)
                run(V_RET, p, 40, 40, {16: [lambda: relu(0)], 18: [lambda: relu(1)], 20: [lambda: relu(2)],
                                       22: [lambda: relu(3)], 24: [lambda: decay_of(0)],
                                       31: [lambda: decay_of(1)], 35: [tanh]})

            ret_turn(0)
            with act.Fori(1, NPAIR) as p:
                ret_turn(p)
            up_phase(V_UPR, N_UPR, 8, 4 + 8, None)

            def dsa_turn(p):
                def exps(a):
                    act.wait_ge(neg_max, MEM_HEADS + 2 * p + a + 1)
                    for b in range(TT):
                        part = pr[a][:, ROW_AT[b]:ROW_AT[b] + P * (b + 1)]
                        ins = nc.scalar.activation(part, part, ACT.Exp, bias=rmax[:, a, b:b + 1],
                                                   accum_out=rsum[:, a, b:b + 1])
                    ins.then_inc(exp_done, 1)

                def tanh():
                    at_least(act, y_done, 12 + 2 * p)
                    tanh_gate(0, V_DSA + 24 + 32 * p)
                run(V_DSA, p, 32, 32, {23: [lambda: exps(0)], 26: [lambda: exps(1)], 27: [tanh]})

            dsa_turn(0)
            with act.Fori(1, NPAIR) as p:
                dsa_turn(p)
            up_phase(V_UPD, N_UPD, 16, 4 + 16, None)

            def m_split(k):
                act.wait_ge(z_done, N_OUT - 2 if k < KT - 2 else N_OUT)
                act.wait_ge(half_used, V_OUT - 4)
                nc.scalar.activation(m_hi[:, k, :], merged[:, k, :], ACT.Copy).then_inc(m_hi_done, 1)

            def out_squares(g):
                act.wait_ge(half_used, V_OUT + 16 * g + 16)
                for t in range(TT):
                    ins = nc.scalar.activation(sq_out[:, 0:512], ps[:, 4 * ((g + 1) % 2) + t, :], ACT.Square,
                                               accum_out=ssq[:, t, g:g + 1])
                    ins.then_inc(out_sq, 1)
                    act.wait_ge(out_sq, 4 * g + t + 1)

            for k in range(KT // 4):
                m_split(k)
            first = {k: [lambda k=k: m_split(KT // 4 + k)] for k in range(3 * KT // 4)}
            run(V_OUT, 0, 16, 16, first)
            for g in range(1, 4):
                run(V_OUT, g, 16, 16, {4: [lambda: out_squares(g - 1)]})
            out_squares(3)

        @block.tensor
        def _(pe):
            def three(dst, w_at, m_hi_ap, m_lo_ap, first, last, skip=False):
                nc.tensor.matmul(dst, w_at(w_hi), m_hi_ap, start=first, stop=False, skip_group_check=skip)
                nc.tensor.matmul(dst, w_at(w_hi), m_lo_ap, start=False, stop=False, skip_group_check=skip)
                return nc.tensor.matmul(dst, w_at(w_lo), m_hi_ap, start=False, stop=last, skip_group_check=skip)

            def transposed(bank, count, rhs_hi, rhs_lo, cols=SEQ, m=P, tiles=2):
                def product(k, s):
                    for kk in range(2):
                        kt = 2 * k + kk
                        for i in range(tiles):
                            last = three(ps[0:m, bank + i, 0:cols],
                                         lambda w: w[:, s, kk, P * i:P * i + m],
                                         rhs_hi[:, kt, :], rhs_lo[:, kt, :], kt == 0, kt == 2 * count - 1)
                    return last
                return product

            def in_rows(bank, lhs_hi, lhs_lo, tiles, per_bank):
                def product(k, s):
                    for kk in range(2):
                        kt = 2 * k + kk
                        for t in range(tiles):
                            dst = ps[:, bank + t // per_bank, GC * (t % per_bank):GC * (t % per_bank) + GC]
                            tok = slice(P * t, P * t + P)
                            nc.tensor.matmul(dst, lhs_hi[:, kt, tok], w_hi[:, s, kk, :],
                                             start=(kt == 0 and t % per_bank == 0), stop=False,
                                             skip_group_check=True)
                            nc.tensor.matmul(dst, lhs_lo[:, kt, tok], w_hi[:, s, kk, :],
                                             start=False, stop=False, skip_group_check=True)
                            last = nc.tensor.matmul(dst, lhs_hi[:, kt, tok], w_lo[:, s, kk, :],
                                                    start=False, stop=kt == KT - 1, skip_group_check=True)
                    return last
                return product

            def group(v, g, product, hooks={}, at=0, count=8, banks_free=True):
                if banks_free:
                    at_least(pe, z_done, g - 1)
                for k in range(count):
                    pe.wait_ge(lo_ready, v + k + 1)
                    last = product(k, (at + k) % 4)
                    last.then_inc(half_used, 1)
                    for f in hooks.get(at + k, ()):
                        f()

            pe.wait_ge(small_in, 48)
            pe.wait_ge(consts, 11)
            nc.tensor.transpose(ps[:, 7, 0:40], norm_rows[0:40, :], ident[0:40, 0:40]).then_inc(norm_t, 1)

            def rows_over(n):
                k = n % KT
                rows, tiles, bank, held = ((mem_rows, MT, k % 8, n - 7) if n < KT else
                                           (x_rows, TT, 4 + k % 4, max(n - 3, KT)))
                pe.wait_ge(row_scaled, MT if n < KT else MT + TT)
                if bank == 7:
                    pe.wait_ge(norm_ready, 1)
                at_least(pe, t_lo, held)
                for t in range(tiles):
                    last = nc.tensor.transpose(ps[:, bank, P * t:P * t + P],
                                               rows[:, t, P * k:P * k + P], ident[:, :])
                last.then_inc(t_ready, 1)
            for n in range(KT):
                rows_over(n)

            pe.wait_ge(t_lo, KT)
            for g in range(4):
                group(V_KV + 8 * g, N_KV + g, transposed(2 * (g % 2), 8, memt_hi, memt_lo, MEM),
                      {v - 8 * g: [lambda v=v: rows_over(KT + v - 12)] for v in range(8 * g, 8 * g + 8)
                       if 12 <= v < 12 + KT})
            with pe.Fori(2, 4) as i:
                for e in range(2):
                    group(V_KV + 16 * i + 8 * e, N_KV + 2 * i + e, in_rows(2 * e, memt_hi, memt_lo, MT, 1))
            pe.wait_ge(t_lo, 2 * KT)

            proj = lambda bank: transposed(bank, 8, h_hi, h_lo)

            def mem_logits(h):
                pe.wait_ge(z_done, N_MEM + 2 * h + 1)
                at_least(pe, y_done, h)
                for t in range(TT):
                    for c in range(2):
                        last = nc.tensor.matmul(ps[:, 4 + t // 2, MEM * (t % 2):MEM * (t % 2) + MEM],
                                                z[:, 2 + c, P * t:P * t + P], km[:, bass.ds(2 * h + c, 1), :]
                                                .rearrange("p a m -> p (a m)"), start=c == 0, stop=c == 1)
                last.then_inc(logit_full, 1)

            def mem_turn_over(h):
                pe.wait_ge(p_ready, h + 1)
                at_least(pe, pt_ready, h)
                for t in range(TT):
                    for m in range(MT):
                        last = nc.tensor.transpose(ps[:, 6 + m, P * t:P * t + P],
                                                   p_mem[:, t, P * m:P * m + P], ident[:, :])
                last.then_inc(pt_full, 1)

            def mem_out(h):
                pe.wait_ge(pt_ready, h + 1)
                for c in range(2):
                    for m in range(MT):
                        last = nc.tensor.matmul(ps[:, 4 + c, :], v_mem[:, m, P * c:P * c + P],
                                                pt_mem[:, m, :], start=m == 0, stop=m == MT - 1)
                last.then_inc(o_full, 1)

            def mem_turn(h, prev):
                hooks = {0: [lambda: mem_turn_over(h - 1)], 3: [lambda: mem_out(h - 1)]} if prev else {}
                group(V_MEM + 16 * h, N_MEM + 2 * h, proj(0), hooks)
                group(V_MEM + 16 * h + 8, N_MEM + 2 * h + 1, proj(2), {1: [lambda: mem_logits(h)]})

            mem_turn(0, False)
            with pe.Fori(1, MEM_HEADS) as h:
                mem_turn(h, True)

            def up_phase(v0, g0, sig0, y_all, y_last, hooks):
                def up_product(k, s, first=False):
                    if first and k == 3:
                        pe.wait_ge(y_done, y_all)
                    for kk in range(2):
                        kt = 2 * k + kk
                        for i in range(2):
                            last = three(ps[:, 2 + i, :], lambda w: w[:, s, kk, P * i:P * i + P],
                                         y_hi[:, kt, :], y_lo[:, kt, :], kt == 0, kt == 7)
                    return last

                def turn(i, first):
                    for e in range(2):
                        g = g0 + 4 * i + 2 * e
                        v = v0 + 24 * i + 12 * e
                        start = first and e == 0
                        if start:
                            pe.wait_ge(z_done, g - 1)
                        at_least(pe, sig_ready, sig0 + 2 * i + e)
                        group(v, g, proj(0), hooks if start else {}, banks_free=False)
                        if start:
                            pe.wait_ge(y_done, y_all - y_last)
                        group(v + 8, g + 1, lambda k, s: up_product(k, s, start), count=4)
                turn(0, True)
                with pe.Fori(1, 4) as i:
                    turn(i, False)

            up_phase(V_UPM, N_UPM, 0, 4, 1, {0: [lambda: mem_turn_over(3)], 3: [lambda: mem_out(3)]})

            pe.wait_ge(y_done, MEM_HEADS)

            def ikw_product(k, s):
                for kk in range(2):
                    kt = 2 * k + kk
                    last = three(ps[0:IKW, 5, :], lambda w: w[:, s, kk, 0:IKW], h_hi[:, kt, :], h_lo[:, kt, :],
                                 kt == 0, kt == KT - 1)
                return last
            group(V_IKW, N_IKW, ikw_product, banks_free=False)

            def iw_turn_over():
                pe.wait_ge(iwt_ready, 1)
                for t in range(TT):
                    last = nc.tensor.transpose(ps[:, 4, IDX_HEADS * t:IDX_HEADS * t + IDX_HEADS],
                                               iwt[:, P * t:P * t + P], ident[0:IDX_HEADS, 0:IDX_HEADS])
                last.then_inc(iwt_full, 1)

            def idx_scores(p, n):
                pe.wait_ge(z_done, N_RET + 5 * p + 1)
                if n == 0:
                    pe.wait_ge(iw_ready, 1)
                    at_least(pe, var_read, p)
                    at_least(pe, inner_ready, 2 * p)
                at_least(pe, relu_done, 4 * p + n)
                for b in range(TT):
                    w = P * (b + 1)
                    dst, q = flat[:, PACKED + ROW_AT[b]:PACKED + ROW_AT[b] + w], iq[n // 2][:, n % 2, P * b:P * b + P]
                    nc.tensor.matmul(dst, q, ik_hi[:, 0:w], start=True, stop=False)
                    last = nc.tensor.matmul(dst, q, ik_lo[:, 0:w], start=False, stop=True)
                last.then_inc(idx_full, 1)

            def inner(p, a):
                pe.wait_ge(z_done, N_RET + 5 * p + 3)
                pe.wait_ge(relu_done, 4 * p + 4)
                at_least(pe, inner_ready, 2 * p + a)
                for j in range(TT):
                    last = nc.tensor.matmul(flat[:, PACKED + COL_AT[j]:PACKED + COL_AT[j] + SEQ - P * j],
                                            z[:, a, P * j:P * j + P], z[:, 2 + a, P * j:SEQ],
                                            start=True, stop=True)
                last.then_inc(inner_full, 1)

            def weighted_values(bank, weights, a):
                for j in range(TT):
                    last = nc.tensor.matmul(ps[:, bank, P * j:SEQ], z_v[:, j, a, :],
                                            weights[:, COL_AT[j]:COL_AT[j] + SEQ - P * j],
                                            start=j == 0, stop=j == TT - 1)
                return last

            def ret_out(p):
                pe.wait_ge(z_done, N_RET + 5 * p + 5)
                pe.wait_ge(inner_ready, 2 * p + 2)
                for a in range(2):
                    weighted_values(4 + a, sm[a], a).then_inc(ret_full, 1)

            def ret_var(p):
                pe.wait_ge(sq_ready, p + 1)
                for a in range(2):
                    last = nc.tensor.matmul(ps[:, 4 + a, :], ones[:, :], z[:, a, :], start=True, stop=True)
                last.then_inc(var_full, 1)

            def ret_turn(p, prev):
                g, v = N_RET + 5 * p, V_RET + 40 * p
                tail = {1: [lambda: ret_out(p - 1)], 3: [lambda: ret_var(p - 1)]} if prev else {1: [iw_turn_over]}
                at_least(pe, inner_ready, 2 * p)
                if not prev:
                    pe.wait_ge(pt_ready, MEM_HEADS)
                    pe.wait_ge(sig_ready, 8)
                group(v, g, proj(6), tail, banks_free=False)
                group(v + 8, g + 1, proj(0), {4: [lambda: idx_scores(p, 0)], 6: [lambda: idx_scores(p, 1)]},
                      banks_free=True)
                at_least(pe, z_done, g)
                group(v + 16, g + 2, proj(2), {0: [lambda: idx_scores(p, 2)], 2: [lambda: idx_scores(p, 3)]},
                      banks_free=False)
                pe.wait_ge(z_done, g + 2)
                group(v + 24, g + 3, proj(0), {1: [lambda: inner(p, 0)], 4: [lambda: inner(p, 1)]})
                pe.wait_ge(z_done, g + 3)
                group(v + 32, g + 4, in_rows(2, h_hi, h_lo, TT, 2))

            ret_turn(0, False)
            with pe.Fori(1, NPAIR) as p:
                ret_turn(p, True)
            up_phase(V_UPR, N_UPR, 8, 12, 2, {1: [lambda: ret_out(3)], 3: [lambda: ret_var(3)]})

            def dsa_logits(p, a):
                pe.wait_ge(z_done, N_DSA + 4 * p + 2)
                at_least(pe, logit_read, MEM_HEADS + 2 * p + a)
                at_least(pe, pt_ready, MEM_HEADS + 2 * p)
                at_least(pe, y_done, 12 + 2 * p)
                for b in range(TT):
                    w = P * (b + 1)
                    last = nc.tensor.matmul(flat[:, PACKED + ROW_AT[b]:PACKED + ROW_AT[b] + w],
                                            z[:, 2 + a, P * b:P * b + P], z[:, a, 0:w], start=True, stop=True)
                last.then_inc(logit_full, 1)

            def dsa_turn_over(p, a):
                pe.wait_ge(p_ready, MEM_HEADS + 2 * p + a + 1)
                pe.wait_ge(pt_ready, MEM_HEADS + 2 * p + a)
                for j in range(TT):
                    for b in range(j, TT):
                        at = PACKED + COL_AT[j] + P * (b - j)
                        last = nc.tensor.transpose(flat[:, at:at + P],
                                                   pr[a][:, ROW_AT[b] + P * j:ROW_AT[b] + P * j + P], ident[:, :])
                last.then_inc(pt_full, 1)

            def dsa_out(p, a):
                pe.wait_ge(z_done, N_DSA + 4 * p + 4)
                pe.wait_ge(pt_ready, MEM_HEADS + 2 * p + 2)
                weighted_values((7, 4)[a], pt[a], a).then_inc(o_full, 1)

            def dsa_turn(p, prev):
                g, v = N_DSA + 4 * p, V_DSA + 32 * p
                tail = {1: [lambda: dsa_out(p - 1, 0)], 3: [lambda: dsa_out(p - 1, 1)]} if prev else {}
                if not prev:
                    pe.wait_ge(sig_ready, 16)
                group(v, g, proj(0), tail, banks_free=prev)
                group(v + 8, g + 1, proj(2))
                group(v + 16, g + 2, proj(0), {1: [lambda: dsa_logits(p, 0)], 4: [lambda: dsa_logits(p, 1)]})
                group(v + 24, g + 3, in_rows(2, h_hi, h_lo, TT, 2),
                      {2: [lambda: dsa_turn_over(p, 0)], 5: [lambda: dsa_turn_over(p, 1)]})

            dsa_turn(0, False)
            with pe.Fori(1, NPAIR) as p:
                dsa_turn(p, True)
            up_phase(V_UPD, N_UPD, 16, 20, 2, {1: [lambda: dsa_out(3, 0)], 3: [lambda: dsa_out(3, 1)]})

            pe.wait_ge(sig_ready, 24)
            for g in range(4):
                at_least(pe, out_done, 4 * (g - 1))
                if g == 1:
                    pe.wait_ge(z_done, N_OUT)
                for k in range(16):
                    pe.wait_ge(lo_ready, V_OUT + 16 * g + k + 1)
                    if g == 0:
                        pe.wait_ge(m_lo_done, k + 1)
                    s = k % 4
                    wh = w_hi[:, s, :, :].rearrange("p a n -> p (a n)")
                    wl = w_lo[:, s, :, :].rearrange("p a n -> p (a n)")
                    for t in range(TT):
                        dst, tok = ps[:, 4 * ((g + 1) % 2) + t, :], slice(P * t, P * t + P)
                        nc.tensor.matmul(dst, m_hi[:, k, tok], wh, start=k == 0, stop=False)
                        nc.tensor.matmul(dst, m_lo[:, k, tok], wh, start=False, stop=False)
                        last = nc.tensor.matmul(dst, m_hi[:, k, tok], wl, start=False, stop=k == 15)
                    last.then_inc(half_used, 1)

        @block.vector
        def _(dve):
            st = Steps(dve, own)
            V = nc.vector

            def rsqrt(a, y, u):
                st.then(V.tensor_scalar(u.bitcast(I32), a.bitcast(I32), 1, None, ALU.logical_shift_right))
                st.then(V.tensor_scalar(y.bitcast(I32), u.bitcast(I32), -1.0, RSQRT_SEED, ALU.mult, ALU.add))
                for _ in range(3):
                    st.then(V.scalar_tensor_tensor(out=u, in0=y, scalar=-0.5, in1=y, op0=ALU.mult, op1=ALU.mult))
                    st.then(V.tensor_tensor(u, u, a, ALU.mult))
                    st.then(V.scalar_tensor_tensor(out=y, in0=u, scalar=1.5, in1=y, op0=ALU.add, op1=ALU.mult))

            dve.wait_ge(norm_t, 1)
            V.tensor_copy(norm_w[:, 0:32], ps[:, 7, 0:32])
            V.tensor_scalar(norm_w[:, 32:40], ps[:, 7, 32:40], 0.25, None, ALU.mult).then_inc(norm_ready, 1)
            V.memset(stat[:, 1:3, :], 1.0)
            dve.wait_ge(consts, 11)
            V.tensor_scalar(negtri[:, :], iota_f[:, 0:P], 0.0, NEG, ALU.is_gt, ALU.mult)

            def square_sum(rows, col):
                V.tensor_tensor_reduce(out=junk[:, :], in0=rows, in1=rows, scale=1.0, scalar=0.0, op0=ALU.mult,
                                       op1=ALU.add, accum_out=stat[:, 0, col:col + 1]).then_inc(sq_rows, 1)

            def scale_rows(rows, c0, n):
                part = slice(c0, c0 + n)
                st.then(V.tensor_scalar(stat[:, 0, part], stat[:, 0, part], 1.0 / D, EPS, ALU.mult, ALU.add))
                rsqrt(stat[:, 0, part], stat[:, 1, part], stat[:, 2, part])
                for t in range(n):
                    V.tensor_scalar(rows[:, t, :], rows[:, t, :], stat[:, 1, c0 + t:c0 + t + 1], None,
                                    ALU.mult).then_inc(row_scaled, 1)

            def rows_lo(n):
                dve.wait_ge(t_hi, n + 1)
                k = n % KT
                hi_t, lo_t, bank, cols, col = ((memt_hi, memt_lo, k % 8, MEM, KT + k) if n < KT else
                                               (h_hi, h_lo, 4 + k % 4, SEQ, k))
                V.scalar_tensor_tensor(out=lo_t[:, k, :], in0=ps[:, bank, 0:cols], scalar=norm_w[:, col:col + 1],
                                       in1=hi_t[:, k, :].bitcast(F32), op0=ALU.mult,
                                       op1=ALU.subtract).then_inc(t_lo, 1)

            def take_km(g):
                dve.wait_ge(half_used, V_KV + 8 + 8 * g)
                V.tensor_copy(km[:, 2 * g:2 * g + 2, :],
                              ps[:, 2 * (g % 2):2 * (g % 2) + 2, 0:MEM]).then_inc(z_done, 1)

            def take_vm(i, e):
                dve.wait_ge(half_used, V_KV + 8 + 8 * e + 16 * i)
                V.tensor_scalar(vm[:, :, bass.ds(GC * 2 * (i - 2) + GC * e, GC)], ps[:, 2 * e:2 * e + 2, 0:GC],
                                0.25, None, ALU.mult).then_inc(z_done, 1)

            dve.wait_ge(mem_in[1], 16)
            square_sum(mem_rows[:, 1, :], 5)
            dve.wait_ge(sq_rows, 1)
            dve.wait_ge(sq_done, 1)
            scale_rows(mem_rows, 4, MT)
            for n in range(KT):
                rows_lo(n)
            for t in range(TT):
                dve.wait_ge(x_in[t], 16)
                dve.wait_ge(sq_rows, 1 + t)
                square_sum(x_rows[:, t, :], t)
                if t == 2:
                    take_km(0)
            dve.wait_ge(sq_rows, 1 + TT)
            scale_rows(x_rows, 0, TT)
            for n in range(KT, 2 * KT):
                if n in (KT + 4, KT + 12):
                    take_km(1 if n == KT + 4 else 2)
                rows_lo(n)
            take_km(3)
            with dve.Fori(2, 4) as i:
                take_vm(i, 0)
                take_vm(i, 1)

            def silu_gate(bank, tanhs):
                dve.wait_ge(tanh_done, tanhs)
                ins = V.scalar_tensor_tensor(out=z[:, 4:6, :], in0=z[:, 4:6, :], scalar=1.0,
                                             in1=ps[:, bank:bank + 2, :], op0=ALU.add, op1=ALU.mult)
                ins.then_inc(z_done, 1)
                st.then(V.tensor_copy(top8[:, 0:1], logg[:, 0:1]))

            def mem_finish(h):
                silu_gate(2, h + 1)
                st.then(V.tensor_copy(v_mem[:, :, :], vm[:, :, bass.ds(MEM_HD * h, MEM_HD)]))
                dve.wait_ge(pt_full, h + 1)
                V.tensor_copy(pt_mem[:, :, :], ps[:, 6:8, :]).then_inc(pt_ready, 1)
                dve.wait_ge(o_full, h + 1)
                write_y(2 * h, ps[:, 4:6, :], z[:, 4:6, :], z[:, 0:2, :], 1)

            def write_y(tile, a, b, tmp, signals):
                w = tmp.shape[1]
                dst_hi, dst_lo = y_hi[:, bass.ds(tile, w), :], y_lo[:, bass.ds(tile, w), :]
                st.then(V.tensor_tensor(tmp, a, b, ALU.mult))
                st.then(V.tensor_copy(dst_hi, tmp))
                V.tensor_tensor(dst_lo, tmp, dst_hi.bitcast(F32), ALU.subtract).then_inc(y_done, signals)

            def mem_turn(h, prev):
                if prev:
                    mem_finish(h - 1)
                dve.wait_ge(half_used, V_MEM + 8 + 16 * h)
                V.tensor_scalar(z[:, 2:4, :], ps[:, 0:2, :], MEM_HD ** -0.5, None, ALU.mult).then_inc(z_done, 1)
                dve.wait_ge(logit_full, h + 1)
                st.then(V.tensor_copy(p_mem[:, :, :].rearrange("p t m -> p (t m)"), flat[:, 2048:3072]))
                V.tensor_reduce(rmax[:, 0, :], p_mem[:, :, :], AX.X, ALU.max, negate=True).then_inc(neg_max, 1)
                V.tensor_copy(top8[:, 0:1], logg[:, 0:1]).then_inc(logit_read, 1)
                dve.wait_ge(exp_done, h + 1)
                st.then(V.reciprocal(rinv[:, 0, :], rsum[:, 0, :]))
                for b in range(TT):
                    ins = V.tensor_scalar(p_mem[:, b, :], p_mem[:, b, :], rinv[:, 0, b:b + 1], None, ALU.mult)
                ins.then_inc(p_ready, 1)

            mem_turn(0, False)
            with dve.Fori(1, MEM_HEADS) as h:
                st.enter(h, 1, 6)
                mem_turn(h, True)
                st.leave(MEM_HEADS - 1, 6)

            def up_phase(v0, g0, sig0, first_branch, finish, extra=None, per=0, last_turn=None):
                def turn(i, first):
                    for e in range(2):
                        g = g0 + 4 * i + 2 * e
                        if first and e == 0:
                            finish()
                        if last_turn and isinstance(i, int) and i == 3 and e == 1:
                            last_turn()
                        dve.wait_ge(half_used, v0 + 12 + 12 * e + 24 * i)
                        dve.wait_ge(sig_ready, sig0 + 2 * i + e + 1)
                        tiles = merged[:, bass.ds(4 * i + 2 * e, 2), :]
                        if first_branch:
                            V.scalar_tensor_tensor(out=tiles, in0=z[:, 0:2, :], scalar=1.0, in1=ps[:, 2:4, :],
                                                   op0=ALU.add, op1=ALU.mult).then_inc(z_done, 2)
                        else:
                            st.then(V.scalar_tensor_tensor(out=z[:, 2:4, :], in0=z[:, 0:2, :], scalar=1.0,
                                                           in1=ps[:, 2:4, :], op0=ALU.add, op1=ALU.mult))
                            V.tensor_tensor(tiles, tiles, z[:, 2:4, :], ALU.add).then_inc(z_done, 2)
                        if extra:
                            extra(i, e)
                turn(0, True)
                if last_turn:
                    with dve.Fori(1, 3) as i:
                        st.enter(i, 1, per)
                        turn(i, False)
                        st.leave(2, per)
                    turn(3, False)
                    return
                if extra:
                    for i in range(1, 4):
                        turn(i, False)
                    return
                with dve.Fori(1, 4) as i:
                    st.enter(i, 1, per)
                    turn(i, False)
                    st.leave(3, per)

            up_phase(V_UPM, N_UPM, 0, True, lambda: mem_finish(3))

            dve.wait_ge(half_used, V_IKW + 8)
            ik_psum = ps[0:IDX_DIM, 5, :]
            V.tensor_copy(ik_hi[0:IDX_DIM, :], ik_psum)
            st.then(V.tensor_copy(ik_hi[IDX_DIM:P, :], ik_psum))
            for half in (slice(0, IDX_DIM), slice(IDX_DIM, P)):
                V.tensor_tensor(ik_lo[half, :], ik_psum, ik_hi[0:IDX_DIM, :].bitcast(F32), ALU.subtract)
            V.tensor_scalar(iwt[:, :], ps[IDX_DIM:IKW, 5, :], (IDX_HEADS ** -0.5) * (IDX_DIM ** -0.5), None,
                            ALU.mult).then_inc(iwt_ready, 1)
            V.memset(score[:, :], 0.0).then_inc(z_done, 1)
            dve.wait_ge(iwt_full, 1)
            V.tensor_copy(iw[:, :, :].rearrange("p t h -> p (t h)"),
                          ps[:, 4, 0:TT * IDX_HEADS]).then_inc(iw_ready, 1)

            def ret_finish(p):
                o, a, y, u = z[:, 2:4, :], z[:, 0:2, :], z[:, 6:8, :], scratch[:, :, :]
                dve.wait_ge(ret_full, 2 * p + 2)
                st.then(V.tensor_copy(o, ps[:, 4:6, :]))
                V.tensor_tensor(a, o, o, ALU.mult).then_inc(sq_ready, 1)
                dve.wait_ge(var_full, p + 1)
                V.tensor_scalar(a, ps[:, 4:6, :], GN_EPS, None, ALU.add).then_inc(var_read, 1)
                st.then(V.tensor_copy(top8[:, 0:1], logg[:, 0:1]))
                rsqrt(a, y, u)
                for b in range(2):
                    ins = V.scalar_tensor_tensor(out=o[:, b, :], in0=o[:, b, :],
                                                 scalar=norm_w[:, bass.ds(2 * KT + 2 * p + b, 1)],
                                                 in1=y[:, b, :], op0=ALU.mult, op1=ALU.mult)
                st.then(ins)
                write_y(2 * p, o, z[:, 4:6, :], a, 2)

            def ret_turn(p, prev):
                g = N_RET + 5 * p
                if prev:
                    ret_finish(p - 1)
                dve.wait_ge(half_used, V_RET + 8 + 40 * p)
                for n in range(4):
                    src = ps[IDX_DIM * (n % 2):IDX_DIM * (n % 2) + IDX_DIM, 6 + n // 2, :]
                    ins = V.tensor_copy(iq[n // 2][0:IDX_DIM, n % 2, :], src)
                st.then(ins)
                for n in range(4):
                    src = ps[IDX_DIM * (n % 2):IDX_DIM * (n % 2) + IDX_DIM, 6 + n // 2, :]
                    ins = V.tensor_tensor(iq[n // 2][IDX_DIM:P, n % 2, :], src,
                                          iq[n // 2][0:IDX_DIM, n % 2, :].bitcast(F32), ALU.subtract)
                ins.then_inc(z_done, 1)
                dve.wait_ge(half_used, V_RET + 16 + 40 * p)
                V.tensor_scalar(z[:, 0:2, :], ps[:, 0:2, :], HD ** -0.5, None, ALU.mult).then_inc(z_done, 1)
                for n in range(4):
                    dve.wait_ge(relu_done, 4 * p + n + 1)
                    for b in range(TT):
                        w = P * (b + 1)
                        part = slice(ROW_AT[b], ROW_AT[b] + w)
                        ins = V.scalar_tensor_tensor(out=score[:, part], in0=sm[n % 2][:, part],
                                                     scalar=iw[:, b, bass.ds(4 * p + n, 1)], in1=score[:, part],
                                                     op0=ALU.mult, op1=ALU.add)
                    ins.then_inc(relu_used, 1)
                    if n == 3:
                        dve.wait_ge(half_used, V_RET + 24 + 40 * p)
                        V.tensor_copy(z[:, 2:4, :], ps[:, 2:4, :]).then_inc(z_done, 1)
                    dve.wait_ge(relu_used, 4 * p + n + 1)
                for a in range(2):
                    dve.wait_ge(decay_ready, 2 * p + a + 1)
                    st.then(V.scalar_tensor_tensor(out=decay[:, 0:P], in0=iota_f[:, 0:P], scalar=0.0,
                                                   in1=decay[:, 0:P], op0=ALU.is_ge, op1=ALU.mult))
                    dve.wait_ge(inner_full, 2 * p + a + 1)
                    for j in range(TT):
                        w = SEQ - P * j
                        at = COL_AT[j]
                        ins = V.tensor_tensor(sm[a][:, at:at + w], flat[:, PACKED + at:PACKED + at + w],
                                              decay[:, 0:w], ALU.mult)
                    ins.then_inc(inner_ready, 1)
                silu_gate(0, MEM_HEADS + p + 1)
                dve.wait_ge(half_used, V_RET + 40 + 40 * p)
                rows = flat[:, 1024:2048].rearrange("p (t h d) -> p (t h) d", h=2, d=HD)
                st.then(V.tensor_reduce(stat[:, 0, :], rows, AX.X, ALU.add))
                st.then(V.tensor_scalar(stat[:, 0, :], stat[:, 0, :], 1.0 / HD, None, ALU.mult))
                V.tensor_tensor(z_v.rearrange("p t h d -> p (t h) d"), rows,
                                stat[:, 0, :].unsqueeze(2).to_broadcast([P, 8, HD]),
                                ALU.subtract).then_inc(z_done, 1)

            RET_STEPS = 22
            ret_turn(0, False)
            with dve.Fori(1, NPAIR) as p:
                st.enter(p, 1, RET_STEPS)
                ret_turn(p, True)
                st.leave(NPAIR - 1, RET_STEPS)

            def select_keys(b, e):
                w = P * (b + 1)
                part = slice(ROW_AT[b], ROW_AT[b] + w)
                row = score[:, part]
                if w > TOPK:
                    if e == 0:
                        st.then(V.tensor_copy(top8[:, 0:1], logg[:, 0:1]))
                    for _ in range(TOPK // 16):
                        st.then(V.max(out=top8[:, :], in_=row))
                        st.then(V.match_replace(out=row, in_to_replace=top8[:, :], in_values=row, imm_value=TAKEN))
                if e == 1:
                    if w > TOPK:
                        st.then(V.tensor_scalar(row, row, TAKEN / 2, FAR, ALU.is_gt, ALU.mult))
                    else:
                        st.then(V.memset(row, 0.0))
                    st.then(V.tensor_tensor(row, row, iota_f[:, 0:w], ALU.subtract))
                    st.then(V.tensor_scalar(far[:, part], row, float(P * b), None, ALU.add))

            def ret_end():
                ret_finish(3)
                for b in range(TT):
                    d = score[:, ROW_AT[b] + P * b:ROW_AT[b] + P * b + P]
                    V.tensor_tensor(d, d, negtri[:, :], ALU.add)

            up_phase(V_UPR, N_UPR, 8, False, ret_end, select_keys)
            for b in range(TT):
                d = far[:, ROW_AT[b] + P * b:ROW_AT[b] + P * b + P]
                st.then(V.scalar_tensor_tensor(out=d, in0=negtri[:, :], scalar=FAR / NEG, in1=d,
                                               op0=ALU.mult, op1=ALU.add))

            def dsa_finish(p):
                for a in range(2):
                    dve.wait_ge(o_full, MEM_HEADS + 2 * p + a + 1)
                    write_y(2 * p + a, ps[:, (7, 4)[a]:(7, 4)[a] + 1, :], z[:, 4 + a:5 + a, :], z[:, 3:4, :], 1)
                    st.then(V.tensor_copy(top8[:, 0:1], logg[:, 0:1]))

            def dsa_turn(p, prev):
                g = N_DSA + 4 * p
                if prev:
                    dsa_finish(p - 1)
                dve.wait_ge(half_used, V_DSA + 8 + 32 * p)
                V.tensor_scalar(z[:, 0:2, :], ps[:, 0:2, :], HD ** -0.5, None, ALU.mult).then_inc(z_done, 1)
                dve.wait_ge(half_used, V_DSA + 16 + 32 * p)
                V.tensor_copy(z[:, 2:4, :], ps[:, 2:4, :]).then_inc(z_done, 1)
                for a in range(2):
                    dve.wait_ge(logit_full, MEM_HEADS + 2 * p + a + 1)
                    for b in range(TT):
                        w, at = P * (b + 1), ROW_AT[b]
                        ins = V.scalar_tensor_tensor(out=pr[a][:, at:at + w], in0=far[:, at:at + w],
                                                     scalar=slope[:, bass.ds(2 * p + a, 1)],
                                                     in1=flat[:, PACKED + at:PACKED + at + w],
                                                     op0=ALU.mult, op1=ALU.add)
                    ins.then_inc(logit_read, 1)
                    dve.wait_ge(logit_read, MEM_HEADS + 2 * p + a + 1)
                    for b in range(TT):
                        w, at = P * (b + 1), ROW_AT[b]
                        ins = V.tensor_reduce(rmax[:, a, b:b + 1], pr[a][:, at:at + w], AX.X, ALU.max, negate=True)
                    ins.then_inc(neg_max, 1)
                for a in range(2):
                    dve.wait_ge(exp_done, MEM_HEADS + 2 * p + a + 1)
                    st.then(V.reciprocal(rinv[:, a, :], rsum[:, a, :]))
                    for b in range(TT):
                        w, at = P * (b + 1), ROW_AT[b]
                        ins = V.tensor_scalar(pr[a][:, at:at + w], pr[a][:, at:at + w], rinv[:, a, b:b + 1], None,
                                              ALU.mult)
                    ins.then_inc(p_ready, 1)
                for a in range(2):
                    dve.wait_ge(pt_full, MEM_HEADS + 2 * p + a + 1)
                    V.tensor_copy(pt[a][:, :], flat[:, PACKED:PACKED + PACK]).then_inc(pt_ready, 1)
                    if a == 0:
                        silu_gate(0, MEM_HEADS + NPAIR + p + 1)
                dve.wait_ge(half_used, V_DSA + 32 + 32 * p)
                V.tensor_scalar(z_v.rearrange("p t h d -> p (t h d)"), flat[:, 1024:2048], 0.25, None,
                                ALU.mult).then_inc(z_done, 1)

            DSA_STEPS = 9
            dsa_turn(0, False)
            with dve.Fori(1, NPAIR) as p:
                st.enter(p, 1, DSA_STEPS)
                dsa_turn(p, True)
                st.leave(NPAIR - 1, DSA_STEPS)

            def merged_lo(k):
                dve.wait_ge(m_hi_done, k + 1)
                V.tensor_tensor(m_lo[:, k, :], merged[:, k, :], m_hi[:, k, :].bitcast(F32),
                                ALU.subtract).then_inc(m_lo_done, 1)

            up_phase(V_UPD, N_UPD, 16, False, lambda: dsa_finish(3), None, 2,
                     lambda: [merged_lo(k) for k in range(KT // 4)])
            for k in range(KT // 4, KT):
                merged_lo(k)
            dve.wait_ge(post_in, 16)
            for g in range(4):
                for t in range(TT):
                    dve.wait_ge(out_sq, 4 * g + t + 1)
                    V.tensor_tensor(o_rows[:, t, 512 * g:512 * g + 512], ps[:, 4 * ((g + 1) % 2) + t, :],
                                    post_w[:, 512 * g:512 * g + 512], ALU.mult).then_inc(out_done, 1)
            st.then(V.tensor_reduce(stat[:, 0, 0:TT], ssq[:, :, :], AX.X, ALU.add))
            st.then(V.tensor_scalar(stat[:, 0, 0:TT], stat[:, 0, 0:TT], 1.0 / D, EPS, ALU.mult, ALU.add))
            rsqrt(stat[:, 0, 0:TT], stat[:, 1, 0:TT], stat[:, 2, 0:TT])
            dve.wait_ge(again_in, 16)
            for t in range(TT):
                V.scalar_tensor_tensor(out=o_rows[:, t, :], in0=o_rows[:, t, :], scalar=stat[:, 1, t:t + 1],
                                       in1=x_again[:, t, :], op0=ALU.mult, op1=ALU.add).then_inc(final, 1)


_INS = ["x", "mem", "pre_norm_w", "w_in", "ret_gn_w", "mem_norm_w", "w_mem_kv", "w_up_ret", "w_up_dsa",
        "w_up_mem", "w_o", "post_norm_w"]


def kernel(**inputs):
    import numpy as _np
    import concourse.bacc as _bacc
    from concourse import mybir as _mybir
    from concourse.bass_utils import run_bass_kernel_spmd as _run

    nc = _bacc.Bacc("TRN2", target_bir_lowering=False, num_devices=1)
    arrays, args = {}, []
    for name in _INS:
        a = _np.ascontiguousarray(inputs[name])
        arrays[f"in_{name}"] = a
        args.append(nc.dram_tensor(f"in_{name}", a.shape, _mybir.dt.from_np(a.dtype), kind="ExternalInput").ap())
    args.append(nc.dram_tensor("out_0", (1, SEQ, D), F32, kind="ExternalOutput").ap())
    build(nc, *args)
    r = _run(nc, [arrays], core_ids=[0])
    return r.results[0]["out_0"]
```

```python
from contextlib import ExitStack

import numpy as np

import concourse.bass as bass
from concourse import mybir

F32 = mybir.dt.float32
F32R = mybir.dt.float32r
I32 = mybir.dt.int32
ALU = mybir.AluOpType
ACT = mybir.ActivationFunctionType
AX = mybir.AxisListType

P = 128
SEQ = 512
D = 2048
KT = D // P
TT = SEQ // P
MEM = 256
MT = MEM // P
MEM_PART = D // 4
HD = 128
WIDTH = 1024
NPAIR = WIDTH // 256
IDX_HEADS = 16
IDX_DIM = 64
TOPK = min(256, SEQ // 4)
MEM_HEADS = 4
MEM_HD = 256
GC = 256
EPS = 1e-6
GN_EPS = 1e-5
NEG = -1e30
TAKEN = -3e38
FAR = 1e32
RSQRT_SEED = float(0x5F3759DF)

RQ, RK, RV, RG, AQ, AK, AV, AG, IQ, IK = [WIDTH * n for n in range(10)]
IKW = IDX_DIM + IDX_HEADS
MQ = IK + IKW
MG = MQ + WIDTH
G_RET = MG + WIDTH
G_DSA = G_RET + D
G_MEM = G_DSA + D

ROW_AT = {0: 896, 1: 1024, 2: 512, 3: 0}
COL_AT = {0: 0, 1: 512, 2: 1024, 3: 896}
PACK = 1280

V_KV, V_MEM = 0, 64
V_UPM = V_MEM + 4 * 16
V_IKW = V_UPM + 8 * 12
V_RET = V_IKW + 8
V_UPR = V_RET + 4 * 40
V_DSA = V_UPR + 8 * 12
V_UPD = V_DSA + 4 * 32
V_OUT = V_UPD + 8 * 12
V_END = V_OUT + 4 * 16
X_OVER = [22, 22, 22, 23, 23, 24, 24, 25, 25, 25, 26, 26, 27, 27, 28, 28]
RMS_OVER = 3
LAST_HALVES = 3
N_KV, N_MEM, N_UPM, N_IKW, N_RET = 0, 8, 16, 32, 33
N_UPR = N_RET + 20
N_DSA = N_UPR + 16
N_UPD = N_DSA + 16
N_OUT = N_UPD + 16


def at_least(eng, sem, value):
    if isinstance(value, int) and value <= 0:
        return
    eng.wait_ge(sem, value)


class Steps:

    def __init__(self, eng, sem):
        self.eng, self.sem, self.base, self.n = eng, sem, 0, 0

    def then(self, ins):
        self.n += 1
        ins.then_inc(self.sem, 1)
        self.eng.wait_ge(self.sem, self.base + self.n)

    def enter(self, i, first, per):
        self.start = self.base + self.n
        self.base, self.n = self.start + (i - first) * per, 0

    def leave(self, turns, per):
        assert self.n == per, (self.n, per)
        self.base, self.n = self.start + turns * per, 0


def build(nc, x, mem, pre_norm_w, w_in, ret_gn_w, mem_norm_w, w_mem_kv, w_up_ret, w_up_dsa,
          w_up_mem, w_o, post_norm_w, out):
    with ExitStack() as ctx:
        base = 16640
        used = [base]

        def place(name, shape, dt=F32, at=None):
            size = 4 * int(np.prod(shape[1:]))
            if at is None:
                at = used[0]
                used[0] += (size + 31) // 32 * 32
            return nc.alloc_sbuf_tensor_at(name, shape, dt, offset=at), at

        def sem(name):
            return ctx.enter_context(nc.semaphore(name))

        h_hi, at_h = place("h_hi", [P, KT, SEQ], F32R)
        h_lo, at_hl = place("h_lo", [P, KT, SEQ], F32R)
        raw, _ = place("raw", [P, 4, 4, GC])
        w_hi, _ = place("w_hi", [P, 4, 2, GC], F32R)
        w_lo, _ = place("w_lo", [P, 4, 2, GC], F32R)
        y_hi, at_y = place("y_hi", [P, 8, SEQ], F32R)
        y_lo, _ = place("y_lo", [P, 8, SEQ], F32R)
        merged, at_m = place("merged", [P, KT, SEQ])
        z, at_z = place("z", [P, 8, SEQ])
        z_v = z[:, 6:8, :].rearrange("p a (t d) -> p (a t) d", t=4).rearrange(
            "p (t h) d -> p t h d", h=2)
        far, at_far = place("far", [P, 2048])
        iota_f, _ = place("iota_f", [P, SEQ])
        negtri, _ = place("negtri", [P, P])
        ident, _ = place("ident", [P, P])
        ones, _ = place("ones", [P, P])
        logg, _ = place("logg", [P, 8])
        slope, _ = place("slope", [P, 8])
        norm_w, _ = place("norm_w", [P, 40])
        stat, _ = place("stat", [P, 3, 8])
        top8, _ = place("top8", [P, 8])
        rmax, _ = place("rmax", [P, 2, 4])
        rsum, _ = place("rsum", [P, 2, 4])
        rinv, _ = place("rinv", [P, 2, 4])
        ssq, _ = place("ssq", [P, TT, 4])
        at_x = used[0]

        x_rows, _ = place("x_rows", [P, TT, D], at=at_m)
        mem_rows, _ = place("mem_rows", [P, MT, D], at=at_z)
        memt_hi, _ = place("memt_hi", [P, KT, MEM], F32R, at=at_y)
        memt_lo, _ = place("memt_lo", [P, KT, MEM], F32R, at=at_y + 16384)
        junk, _ = place("junk", [P, D], at=at_x + 8192)
        junk_act, _ = place("junk_act", [P, D], at=at_h)
        norm_rows, _ = place("norm_rows", [40, P], at=at_x)
        iota_i, _ = place("iota_i", [P, SEQ], I32, at=at_x + 512)
        km_hi, _ = place("km_hi", [P, 8, MEM], F32R, at=at_far)
        km_lo, _ = place("km_lo", [P, 8, MEM], F32R, at=at_x)
        p_mem, _ = place("p_mem", [P, TT, MEM], at=at_x + 8192)
        km_f, _ = place("km_f", [P, 2, MEM], at=at_x + 16384)
        rms_mem, _ = place("rms_mem", [P, MEM], at=at_x + 18432)
        rms_diag, _ = place("rms_diag", [P, MEM], at=at_hl)
        vm, _ = place("vm", [P, MT, WIDTH], at=at_m)
        vh_hi, _ = place("vh_hi", [P, MT, MEM_HD], F32R, at=at_m + 8192)
        vh_lo, _ = place("vh_lo", [P, MT, MEM_HD], F32R, at=at_m + 10240)
        ptm_hi, _ = place("ptm_hi", [P, MT, SEQ], F32R, at=at_m + 12288)
        ptm_lo, _ = place("ptm_lo", [P, MT, SEQ], F32R, at=at_m + 16384)
        mq_hi, _ = place("mq_hi", [P, 2, SEQ], F32R, at=at_m + 20480)
        mq_lo, _ = place("mq_lo", [P, 2, SEQ], F32R, at=at_m + 24576)
        sm_a, _ = place("sm_a", [P, PACK], at=at_far)
        ik_hi, _ = place("ik_hi", [P, SEQ], F32R, at=at_far + 5120)
        iw, _ = place("iw", [P, TT, IDX_HEADS], at=at_far + 7168)
        score, _ = place("score", [P, PACK], at=at_x)
        sm_b, _ = place("sm_b", [P, PACK], at=at_x + 5120)
        iq = [place("iq_a", [P, 2, SEQ], F32R, at=at_x + 10240)[0],
              place("iq_b", [P, 2, SEQ], F32R, at=at_z + 8192)[0]]
        scratch, _ = place("scratch", [P, 2, SEQ], at=at_x + 10240)
        decay, _ = place("decay", [P, SEQ], at=at_x + 14336)
        iwt, _ = place("iwt", [IDX_HEADS, SEQ], at=at_x + 14336)
        ik_lo, _ = place("ik_lo", [P, SEQ], F32R, at=at_x + 16384)
        assert at_x + 19456 <= nc.sbuf_usable_end, (at_x, nc.sbuf_usable_end)
        pr = [place("p_a", [P, PACK], at=at_x)[0], place("p_b", [P, PACK], at=at_x + 5120)[0]]
        pt = [place("pt_a", [P, PACK], at=at_x + 10240)[0], place("pt_b", [P, PACK], at=at_z)[0]]
        m_hi, _ = place("m_hi", [P, KT, SEQ], F32R, at=at_h)
        m_lo, _ = place("m_lo", [P, KT, SEQ], F32R, at=at_hl)
        o_rows, _ = place("o_rows", [P, TT, D], at=at_y)
        x_again, _ = place("x_again", [P, TT, D], at=at_m)
        post_w, _ = place("post_w", [P, D], at=at_far)
        sq_out, _ = place("sq_out", [P, 1024], at=at_x)
        sm = [sm_a, sm_b]

        ps = ctx.enter_context(nc.psum_tensor("ps", [P, 8, 512], F32))
        flat = ps[:, :, :].rearrange("p b n -> p (b n)")
        PACKED = 4 * 512

        raw_in = [sem(f"raw_in{i}") for i in range(4)]
        hi_ready, lo_ready, half_used = sem("hi_ready"), sem("lo_ready"), sem("half_used")
        z_done, sig_ready = sem("z_done"), sem("sig_ready")
        small_in = sem("small_in")
        mem_in, x_in = [sem(f"mem_in{c}") for c in range(4)], [sem(f"x_in{t}") for t in range(TT)]
        consts, pool_own = sem("consts"), sem("pool_own")
        sq_done, sq_rows, row_scaled = sem("sq_done"), sem("sq_rows"), sem("row_scaled")
        t_ready, t_hi, t_lo = sem("t_ready"), sem("t_hi"), sem("t_lo")
        norm_t, norm_ready = sem("norm_t"), sem("norm_ready")
        diag_ready, rms_full = sem("diag_ready"), sem("rms_full")
        rstd_ready, scaled, final_pool = sem("rstd_ready"), sem("scaled"), sem("final_pool")
        logit_full, logit_read, neg_max, exp_done, p_ready = (
            sem("logit_full"), sem("logit_read"), sem("neg_max"), sem("exp_done"), sem("p_ready"))
        pt_full, pt_ready, o_full, y_done, tanh_done = (
            sem("pt_full"), sem("pt_ready"), sem("o_full"), sem("y_done"), sem("tanh_done"))
        iwt_ready, iwt_full, iw_ready = sem("iwt_ready"), sem("iwt_full"), sem("iw_ready")
        idx_full, relu_done, relu_used = sem("idx_full"), sem("relu_done"), sem("relu_used")
        decay_ready, inner_full, inner_ready = sem("decay_ready"), sem("inner_full"), sem("inner_ready")
        ret_full, sq_ready, var_full, var_read = (sem("ret_full"), sem("sq_ready"), sem("var_full"),
                                                  sem("var_read"))
        m_hi_done, m_lo_done = sem("m_hi_done"), sem("m_lo_done")
        out_sq, out_done, tile_whole = sem("out_sq"), sem("out_done"), sem("tile_whole")
        again_in, post_in, final, stored, own = (sem("again_in"), sem("post_in"), sem("final"), sem("stored"),
                                                 sem("own"))

        def by_units(w):
            return w.rearrange("(u t p) n -> u p t n", t=4, p=P)

        win_u, wkv_u = by_units(w_in[0]), by_units(w_mem_kv[0])
        up_u = {"m": by_units(w_up_mem[0]), "r": by_units(w_up_ret[0]), "d": by_units(w_up_dsa[0])}
        wo_u = w_o[0].rearrange("(u t p) n -> u p t n", t=2, p=P)
        x_t = x[0].rearrange("(t p) d -> t p d", p=P)
        mem_t = mem[0].rearrange("(t p) d -> p t d", p=P)
        out_t = out[0].rearrange("(t p) d -> t p d", p=P)

        block = ctx.enter_context(nc.Block())

        @block.sync
        def _(sp):
            def unit(v, slot, src, cols=GC):
                at_least(sp, lo_ready, v - 6)
                sp.dma_start(raw[:, slot, :, 0:cols], src).then_inc(raw_in[slot], 16)

            def group(v, col, view=win_u, slot0=0, cols=GC):
                for u in range(4):
                    unit(v + 2 * u, (slot0 + u) % 4, view[u, :, :, bass.ds(col, cols)], cols)

            def two_units(v, col, view, slot0):
                at_least(sp, lo_ready, v + 2 - 6)
                for u in (1, 0):
                    sp.dma_start(raw[:, slot0 + u, :, :],
                                 view[u, :, :, bass.ds(col, GC)]).then_inc(raw_in[slot0 + u], 16)

            def norm_weights():
                sp.dma_start(norm_rows[0:16, :], pre_norm_w[0].rearrange("(k p) -> k p", p=P)).then_inc(small_in, 16)
                sp.dma_start(norm_rows[16:32, :], mem_norm_w[0].rearrange("(k p) -> k p", p=P)).then_inc(small_in, 16)
                sp.dma_start(norm_rows[32:40, :], ret_gn_w[0].rearrange("(k p) -> k p", p=P)).then_inc(small_in, 16)

            for c in range(4):
                cols = slice(MEM_PART * c, MEM_PART * c + MEM_PART)
                sp.dma_start(mem_rows[:, :, cols], mem_t[:, :, cols]).then_inc(mem_in[c], 16)
                if c == 0:
                    norm_weights()
                unit(V_KV + 2 * c, c, wkv_u[c, :, :, 0:GC])
            for t in range(TT):
                unit(V_KV + 8 + 2 * t, t, wkv_u[t, :, :, GC:2 * GC])
                sp.dma_start(x_rows[:, t, :], x_t[t]).then_inc(x_in[t], 16)
            with sp.Fori(2, 8) as g:
                group(V_KV + 8 * g, g * GC, wkv_u)
            with sp.Fori(0, MEM_HEADS) as h:
                group(V_MEM + 16 * h, MQ + GC * h)
                group(V_MEM + 8 + 16 * h, MG + GC * h)

            def up_phase(v0, gate_col, view):
                with sp.Fori(0, 4) as i:
                    for e in range(2):
                        v = v0 + 24 * i + 12 * e
                        group(v, gate_col + 2 * GC * i + GC * e, slot0=2 * e)
                        two_units(v + 8, 2 * GC * i + GC * e, view, 2 * e)

            up_phase(V_UPM, G_MEM, up_u["m"])
            group(V_IKW, IK, cols=IKW)
            with sp.Fori(0, NPAIR) as p:
                for n, part in enumerate((IQ, RK, RQ, RG, RV)):
                    v = V_RET + 8 * n + 40 * p
                    if part:
                        group(v, part + GC * p)
                    else:
                        two_units(v, part + GC * p, win_u, 0)
                        for u in (2, 3):
                            unit(v + 2 * u, u, win_u[u, :, :, bass.ds(part + GC * p, GC)])
            up_phase(V_UPR, G_RET, up_u["r"])
            with sp.Fori(0, NPAIR) as p:
                for n, part in enumerate((AK, AQ, AG, AV)):
                    group(V_DSA + 8 * n + 32 * p, part + GC * p)
            up_phase(V_UPD, G_DSA, up_u["d"])
            def out_group(g, between=None):
                for u in (1, 0, 2, 3, 4, 5, 6, 7):
                    if u > 0:
                        at_least(sp, lo_ready, V_OUT + 2 * u - 6 + 16 * g)
                    sp.dma_start(raw[:, u % 4, :, :].rearrange("p (t a) n -> p t (a n)", t=2),
                                 wo_u[u, :, :, bass.ds(512 * g, 512)]).then_inc(raw_in[u % 4], 16)
                    if between and u == 4:
                        between()
            out_group(0)
            sp.wait_ge(logit_read, MEM_HEADS + 2 * NPAIR)
            sp.dma_start(post_w[:, :], post_norm_w[0:1, :].broadcast_to([P, D])).then_inc(post_in, 16)

            def x_tile(t):
                sp.wait_ge(m_lo_done, KT)
                sp.dma_start(x_again[:, bass.ds(t, 1), :],
                             x[0, bass.ds(P * t, P), :].unsqueeze(1)).then_inc(again_in, 16)
            with sp.Fori(1, 4) as g:
                out_group(g, lambda: x_tile(g - 1))
            x_tile(TT - 1)
            for n in range(2 * (TT - 1)):
                t, c = n // 2, slice(D // 2 * (n % 2), D // 2 * (n % 2) + D // 2)
                sp.wait_ge(final, n + 1)
                sp.dma_start(out_t[t][:, c], o_rows[:, t, c]).then_inc(stored, 16)
            sp.wait_ge(final_pool, 1)
            sp.dma_start(out_t[TT - 1], o_rows[:, TT - 1, :]).then_inc(stored, 16)
            sp.wait_ge(stored, 16 * (2 * (TT - 1) + 1))

        @block.gpsimd
        def _(pool):
            nc.gpsimd.memset(ident[:, :], 0.0).then_inc(pool_own, 1)
            nc.gpsimd.memset(ones[:, :], 1.0 / HD).then_inc(consts, 1)
            nc.gpsimd.iota(iota_i[:, :], pattern=[[1, SEQ]], base=0, channel_multiplier=-1).then_inc(pool_own, 1)
            pool.wait_ge(pool_own, 2)
            nc.gpsimd.affine_select(out=ident[:, :], in_=ident[:, :], compare_op=ALU.not_equal, fill=1.0,
                                    base=0, pattern=[[-1, P]], channel_multiplier=1).then_inc(consts, 1)
            nc.gpsimd.tensor_copy(iota_f[:, :], iota_i[:, :]).then_inc(consts, 1)
            for h in range(8):
                nc.gpsimd.memset(logg[:, h:h + 1], float(np.log1p(-(2.0 ** (-5.0 - h)))))
                nc.gpsimd.memset(slope[:, h:h + 1], -(2.0 ** (-(h + 1.0)))).then_inc(consts, 1)

            def lo(v, j, cols=GC):
                pool.wait_ge(hi_ready, v + 1)
                s = j % 4
                nc.gpsimd.tensor_tensor(w_lo[:, s, :, 0:cols],
                                        raw[:, (j // 2) % 4, 2 * (j % 2):2 * (j % 2) + 2, 0:cols],
                                        w_hi[:, s, :, 0:cols].bitcast(F32), ALU.subtract).then_inc(lo_ready, 1)

            with pool.Fori(0, (V_IKW - V_KV) // 8) as i:
                for j in range(8):
                    lo(V_KV + 8 * i + j, j)
            for j in range(8):
                lo(V_IKW + j, j, IKW)
            with pool.Fori(0, (V_END - V_RET) // 8) as i:
                for j in range(8):
                    lo(V_RET + 8 * i + j, j)
            pool.wait_ge(scaled, 1)
            pool.wait_ge(again_in, 16 * TT)
            nc.gpsimd.tensor_tensor(o_rows[:, TT - 1, :], o_rows[:, TT - 1, :], x_again[:, TT - 1, :],
                                    ALU.add).then_inc(final_pool, 1)

        @block.scalar
        def _(act):
            def hi(v, j, turn, cols=GC):
                slot = (j // 2) % 4
                act.wait_ge(raw_in[slot], 16 * turn + 16)
                at_least(act, half_used, v - 3)
                nc.scalar.activation(w_hi[:, j % 4, :, 0:cols],
                                     raw[:, slot, 2 * (j % 2):2 * (j % 2) + 2, 0:cols],
                                     ACT.Copy).then_inc(hi_ready, 1)

            def run(first, i, per, count, hooks):
                if isinstance(i, int):
                    v, turn = first + i * per, (first + i * per) // 8
                else:
                    v, turn = first + i * per, first // 8 + i * (per // 8)
                for k in range(count):
                    hi(v + k, k % 8, turn + k // 8)
                    for f in hooks.get(k, ()):
                        f()

            act.wait_ge(consts, 1)
            nc.scalar.activation(junk_act[:, 0:P], ones[:, :], ACT.Copy)

            def rows_hi(n):
                act.wait_ge(t_ready, n + 1)
                k = n % KT
                dst, bank, cols, col = ((memt_hi, 4 + k % 4, MEM, KT + k) if n < KT else
                                        (h_hi, 4 + k % 4, SEQ, k))
                nc.scalar.activation(dst[:, k, :], ps[:, bank, 0:cols], ACT.Copy,
                                     scale=norm_w[:, col:col + 1]).then_inc(t_hi, 1)
            act.wait_ge(norm_ready, 1)

            def x_squares(t):
                act.wait_ge(x_in[t], 16)
                at_least(act, sq_done, t)
                nc.scalar.activation(junk_act[:, :], x_rows[:, t, :], ACT.Square,
                                     accum_out=stat[:, 0, t:t + 1]).then_inc(sq_done, 1)
            for k in range(4):
                rows_hi(k)
            hooks = {7: [lambda: x_squares(0)], 10: [lambda: x_squares(1)], 13: [lambda: x_squares(2)]}
            for c in range(1, 4):
                hooks[2 * c - 1] = [lambda n=n: rows_hi(n) for n in range(4 * c, 4 * c + 4)]
            for k, v in enumerate(X_OVER):
                hooks.setdefault(v + 3, []).append(lambda k=k: rows_hi(KT + k))
            run(V_KV, 0, 32, 32, hooks)
            with act.Fori(4, 8) as g:
                run(V_KV, g, 8, 8, {})

            def tanh_gate(bank, v):
                act.wait_ge(half_used, v)
                nc.scalar.activation(z[:, 4:6, :], ps[:, bank:bank + 2, :], ACT.Tanh,
                                     scale=0.5).then_inc(tanh_done, 1)

            def mem_turn(h, prev):
                def exps():
                    act.wait_ge(logit_read, h + 1)
                    softmax_exp_mem(h)
                hooks = {14: [exps]}
                if prev:
                    hooks[3] = [lambda: mem_tanh(h - 1)]
                run(V_MEM, h, 16, 16, hooks)

            def softmax_exp_mem(h):
                act.wait_ge(neg_max, h + 1)
                for b in range(TT):
                    ins = nc.scalar.activation(p_mem[:, b, :], p_mem[:, b, :], ACT.Exp,
                                               bias=rmax[:, 0, b:b + 1], accum_out=rsum[:, 0, b:b + 1])
                ins.then_inc(exp_done, 1)

            def mem_tanh(h):
                at_least(act, y_done, h)
                tanh_gate(2, V_MEM + 16 + 16 * h)

            mem_turn(0, False)
            with act.Fori(1, MEM_HEADS) as h:
                mem_turn(h, True)

            def up_phase(v0, g0, sig0, y_before, last_tanh):
                def turn(i, first):
                    def sig(e):
                        g = g0 + 4 * i + 2 * e
                        act.wait_ge(half_used, v0 + 8 + 12 * e + 24 * i)
                        act.wait_ge(z_done, g)
                        if first and e == 0:
                            act.wait_ge(y_done, y_before)
                        nc.scalar.activation(z[:, 0:2, :], ps[:, 0:2, :], ACT.Tanh,
                                             scale=0.5).then_inc(sig_ready, 1)
                    hooks = {11: [lambda: sig(0)], 23: [lambda: sig(1)]}
                    if first and last_tanh:
                        hooks[3] = [last_tanh]
                    run(v0, i, 24, 24, hooks)
                turn(0, True)
                with act.Fori(1, 4) as i:
                    turn(i, False)

            up_phase(V_UPM, N_UPM, 0, 4, lambda: mem_tanh(3))

            for j in range(8):
                hi(V_IKW + j, j, V_IKW // 8, IKW)

            def ret_turn(p):
                g0 = N_RET + 5 * p

                def relu(n):
                    act.wait_ge(idx_full, 4 * p + n + 1)
                    at_least(act, relu_used, 4 * p + n - 1)
                    if n < 2:
                        at_least(act, ret_full, 2 * p)
                    nc.scalar.activation(sm[n % 2][:, :], flat[:, PACKED:PACKED + PACK],
                                         ACT.Relu).then_inc(relu_done, 1)

                def decay_of(a):
                    at_least(act, inner_ready, 2 * p + a)
                    nc.scalar.activation(decay[:, :], iota_f[:, :], ACT.Exp,
                                         scale=logg[:, bass.ds(2 * p + a, 1)]).then_inc(decay_ready, 1)

                def tanh():
                    at_least(act, y_done, 4 + 2 * p)
                    tanh_gate(0, V_RET + 32 + 40 * p)
                run(V_RET, p, 40, 40, {17: [lambda: relu(0)], 19: [lambda: relu(1)], 20: [lambda: relu(2)],
                                       22: [lambda: relu(3)], 24: [lambda: decay_of(0)],
                                       31: [lambda: decay_of(1)], 35: [tanh]})

            ret_turn(0)
            with act.Fori(1, NPAIR) as p:
                ret_turn(p)
            up_phase(V_UPR, N_UPR, 8, 4 + 8, None)

            def dsa_turn(p):
                def exps(a):
                    act.wait_ge(neg_max, MEM_HEADS + 2 * p + a + 1)
                    for b in range(TT):
                        part = pr[a][:, ROW_AT[b]:ROW_AT[b] + P * (b + 1)]
                        ins = nc.scalar.activation(part, part, ACT.Exp, bias=rmax[:, a, b:b + 1],
                                                   accum_out=rsum[:, a, b:b + 1])
                    ins.then_inc(exp_done, 1)

                def tanh():
                    at_least(act, y_done, 12 + 2 * p)
                    tanh_gate(0, V_DSA + 24 + 32 * p)
                run(V_DSA, p, 32, 32, {23: [lambda: exps(0)], 26: [lambda: exps(1)], 27: [tanh]})

            dsa_turn(0)
            with act.Fori(1, NPAIR) as p:
                dsa_turn(p)
            up_phase(V_UPD, N_UPD, 16, 4 + 16, None)

            def m_split(k):
                act.wait_ge(z_done, N_OUT - 2 if k < KT - 2 else N_OUT)
                act.wait_ge(half_used, V_OUT - 4)
                nc.scalar.activation(m_hi[:, k, :], merged[:, k, :], ACT.Copy).then_inc(m_hi_done, 1)

            def out_squares(g):
                if g < 3:
                    act.wait_ge(half_used, V_OUT + 16 * g + 16)
                for t in range(TT):
                    if g == 3:
                        act.wait_ge(tile_whole, t + 1)
                    ins = nc.scalar.activation(sq_out[:, 0:512], ps[:, 4 * ((g + 1) % 2) + t, :], ACT.Square,
                                               accum_out=ssq[:, t, g:g + 1])
                    ins.then_inc(out_sq, 1)
                    act.wait_ge(out_sq, 4 * g + t + 1)

            for k in range(KT // 4):
                m_split(k)
            first = {k: [lambda k=k: m_split(KT // 4 + k)] for k in range(3 * KT // 4)}
            run(V_OUT, 0, 16, 16, first)
            for g in range(1, 4):
                run(V_OUT, g, 16, 16, {4: [lambda: out_squares(g - 1)]})
            out_squares(3)
            act.wait_ge(rstd_ready, 1)
            act.wait_ge(out_done, 4 * TT)
            nc.scalar.activation(o_rows[:, TT - 1, :], o_rows[:, TT - 1, :], ACT.Copy,
                                 scale=stat[:, 1, TT - 1:TT]).then_inc(scaled, 1)

        @block.tensor
        def _(pe):
            def three(dst, w_at, m_hi_ap, m_lo_ap, first, last, skip=False):
                nc.tensor.matmul(dst, w_at(w_hi), m_hi_ap, start=first, stop=False, skip_group_check=skip)
                nc.tensor.matmul(dst, w_at(w_hi), m_lo_ap, start=False, stop=False, skip_group_check=skip)
                return nc.tensor.matmul(dst, w_at(w_lo), m_hi_ap, start=False, stop=last, skip_group_check=skip)

            def transposed(bank, count, rhs_hi, rhs_lo, cols=SEQ, m=P, tiles=2):
                def product(k, s):
                    for kk in range(2):
                        kt = 2 * k + kk
                        for i in range(tiles):
                            last = three(ps[0:m, bank + i, 0:cols],
                                         lambda w: w[:, s, kk, P * i:P * i + m],
                                         rhs_hi[:, kt, :], rhs_lo[:, kt, :], kt == 0, kt == 2 * count - 1)
                    return last
                return product

            def in_rows(bank, lhs_hi, lhs_lo, tiles, per_bank):
                def product(k, s):
                    for kk in range(2):
                        kt = 2 * k + kk
                        for t in range(tiles):
                            dst = ps[:, bank + t // per_bank, GC * (t % per_bank):GC * (t % per_bank) + GC]
                            tok = slice(P * t, P * t + P)
                            nc.tensor.matmul(dst, lhs_hi[:, kt, tok], w_hi[:, s, kk, :],
                                             start=(kt == 0 and t % per_bank == 0), stop=False,
                                             skip_group_check=True)
                            nc.tensor.matmul(dst, lhs_lo[:, kt, tok], w_hi[:, s, kk, :],
                                             start=False, stop=False, skip_group_check=True)
                            last = nc.tensor.matmul(dst, lhs_hi[:, kt, tok], w_lo[:, s, kk, :],
                                                    start=False, stop=kt == KT - 1, skip_group_check=True)
                    return last
                return product

            def group(v, g, product, hooks={}, at=0, count=8, banks_free=True):
                if banks_free:
                    at_least(pe, z_done, g - 1)
                for k in range(count):
                    pe.wait_ge(lo_ready, v + k + 1)
                    last = product(k, (at + k) % 4)
                    last.then_inc(half_used, 1)
                    for f in hooks.get(at + k, ()):
                        f()

            def rows_over(n):
                k = n % KT
                rows, tiles, bank, held = ((mem_rows, MT, 4 + k % 4, n - 3) if n < KT else
                                           (x_rows, TT, 4 + k % 4, max(n - 3, KT)))
                if n < KT:
                    pe.wait_ge(mem_in[k // 4], 16)
                else:
                    pe.wait_ge(row_scaled, TT)
                at_least(pe, t_lo, held)
                for t in range(tiles):
                    last = nc.tensor.transpose(ps[:, bank, P * t:P * t + P],
                                               rows[:, t, P * k:P * k + P], ident[:, :])
                last.then_inc(t_ready, 1)
            pe.wait_ge(consts, 2)
            for n in range(4):
                rows_over(n)
            pe.wait_ge(small_in, 48)
            nc.tensor.transpose(ps[:, 0, 0:40], norm_rows[0:40, :], ident[0:40, 0:40]).then_inc(norm_t, 1)
            for n in range(4, 8):
                rows_over(n)

            def rms_over():
                pe.wait_ge(diag_ready, 1)
                nc.tensor.matmul(ps[:, 4, 0:MEM], ones[:, :], rms_diag[:, :], start=True, stop=True)\
                    .then_inc(rms_full, 1)

            for g in range(4):
                hooks = {}
                if g == 0:
                    hooks = {1: [lambda n=n: rows_over(n) for n in range(8, 12)],
                             3: [lambda n=n: rows_over(n) for n in range(12, 16)]}
                elif g == 1:
                    hooks = {RMS_OVER: [rms_over]}
                for k, v in enumerate(X_OVER):
                    if v // 8 == g:
                        hooks.setdefault(v % 8, []).append(lambda k=k: rows_over(KT + k))
                keys = transposed(2 * (g % 2), 8, memt_hi, memt_lo, MEM)

                def product(k, s):
                    if g == 0:
                        pe.wait_ge(t_lo, 2 * k + 2)
                    return keys(k, s)
                group(V_KV + 8 * g, N_KV + g, product, hooks)
            with pe.Fori(2, 4) as i:
                for e in range(2):
                    group(V_KV + 16 * i + 8 * e, N_KV + 2 * i + e, in_rows(2 * e, memt_hi, memt_lo, MT, 1))
            pe.wait_ge(t_lo, 2 * KT)

            proj = lambda bank: transposed(bank, 8, h_hi, h_lo)

            def mem_logits(h):
                pe.wait_ge(z_done, N_MEM + 2 * h + 1)
                at_least(pe, y_done, h)
                for t in range(TT):
                    tok = slice(P * t, P * t + P)
                    dst = ps[:, 4 + t // 2, MEM * (t % 2):MEM * (t % 2) + MEM]
                    for c in range(2):
                        k_hi, k_lo = [k[:, bass.ds(2 * h + c, 1), :].rearrange("p a m -> p (a m)")
                                      for k in (km_hi, km_lo)]
                        nc.tensor.matmul(dst, mq_hi[:, c, tok], k_hi, start=c == 0, stop=False)
                        nc.tensor.matmul(dst, mq_hi[:, c, tok], k_lo, start=False, stop=False)
                        last = nc.tensor.matmul(dst, mq_lo[:, c, tok], k_hi, start=False, stop=c == 1)
                last.then_inc(logit_full, 1)

            def mem_turn_over(h):
                pe.wait_ge(p_ready, h + 1)
                at_least(pe, pt_ready, h)
                for t in range(TT):
                    for m in range(MT):
                        last = nc.tensor.transpose(ps[:, 6 + m, P * t:P * t + P],
                                                   p_mem[:, t, P * m:P * m + P], ident[:, :])
                last.then_inc(pt_full, 1)

            def mem_out(h):
                pe.wait_ge(pt_ready, h + 1)
                for c in range(2):
                    for m in range(MT):
                        dst, col = ps[:, 4 + c, :], slice(P * c, P * c + P)
                        nc.tensor.matmul(dst, vh_hi[:, m, col], ptm_hi[:, m, :], start=m == 0, stop=False)
                        nc.tensor.matmul(dst, vh_hi[:, m, col], ptm_lo[:, m, :], start=False, stop=False)
                        last = nc.tensor.matmul(dst, vh_lo[:, m, col], ptm_hi[:, m, :], start=False,
                                                stop=m == MT - 1)
                last.then_inc(o_full, 1)

            def mem_turn(h, prev):
                hooks = {0: [lambda: mem_turn_over(h - 1)], 3: [lambda: mem_out(h - 1)]} if prev else {}
                group(V_MEM + 16 * h, N_MEM + 2 * h, proj(0), hooks)
                group(V_MEM + 16 * h + 8, N_MEM + 2 * h + 1, proj(2), {1: [lambda: mem_logits(h)]})

            mem_turn(0, False)
            with pe.Fori(1, MEM_HEADS) as h:
                mem_turn(h, True)

            def up_phase(v0, g0, sig0, y_all, y_last, hooks):
                def up_product(k, s, first=False):
                    if first and k == 3:
                        pe.wait_ge(y_done, y_all)
                    for kk in range(2):
                        kt = 2 * k + kk
                        for i in range(2):
                            last = three(ps[:, 2 + i, :], lambda w: w[:, s, kk, P * i:P * i + P],
                                         y_hi[:, kt, :], y_lo[:, kt, :], kt == 0, kt == 7)
                    return last

                def turn(i, first):
                    for e in range(2):
                        g = g0 + 4 * i + 2 * e
                        v = v0 + 24 * i + 12 * e
                        start = first and e == 0
                        if start:
                            pe.wait_ge(z_done, g - 1)
                        at_least(pe, sig_ready, sig0 + 2 * i + e)
                        group(v, g, proj(0), hooks if start else {}, banks_free=False)
                        if start:
                            pe.wait_ge(y_done, y_all - y_last)
                        group(v + 8, g + 1, lambda k, s: up_product(k, s, start), count=4)
                turn(0, True)
                with pe.Fori(1, 4) as i:
                    turn(i, False)

            up_phase(V_UPM, N_UPM, 0, 4, 1, {0: [lambda: mem_turn_over(3)], 3: [lambda: mem_out(3)]})

            pe.wait_ge(y_done, MEM_HEADS)

            def ikw_product(k, s):
                for kk in range(2):
                    kt = 2 * k + kk
                    last = three(ps[0:IKW, 5, :], lambda w: w[:, s, kk, 0:IKW], h_hi[:, kt, :], h_lo[:, kt, :],
                                 kt == 0, kt == KT - 1)
                return last
            group(V_IKW, N_IKW, ikw_product, banks_free=False)

            def iw_turn_over():
                pe.wait_ge(iwt_ready, 1)
                for t in range(TT):
                    last = nc.tensor.transpose(ps[:, 4, IDX_HEADS * t:IDX_HEADS * t + IDX_HEADS],
                                               iwt[:, P * t:P * t + P], ident[0:IDX_HEADS, 0:IDX_HEADS])
                last.then_inc(iwt_full, 1)

            def idx_scores(p, n):
                pe.wait_ge(z_done, N_RET + 5 * p + 1)
                if n == 0:
                    pe.wait_ge(iw_ready, 1)
                    at_least(pe, var_read, p)
                    at_least(pe, inner_ready, 2 * p)
                at_least(pe, relu_done, 4 * p + n)
                for b in range(TT):
                    w = P * (b + 1)
                    dst, q = flat[:, PACKED + ROW_AT[b]:PACKED + ROW_AT[b] + w], iq[n // 2][:, n % 2, P * b:P * b + P]
                    nc.tensor.matmul(dst, q, ik_hi[:, 0:w], start=True, stop=False)
                    last = nc.tensor.matmul(dst, q, ik_lo[:, 0:w], start=False, stop=True)
                last.then_inc(idx_full, 1)

            def inner(p, a):
                pe.wait_ge(z_done, N_RET + 5 * p + 3)
                pe.wait_ge(relu_done, 4 * p + 4)
                at_least(pe, inner_ready, 2 * p + a)
                for j in range(TT):
                    last = nc.tensor.matmul(flat[:, PACKED + COL_AT[j]:PACKED + COL_AT[j] + SEQ - P * j],
                                            z[:, a, P * j:P * j + P], z[:, 2 + a, P * j:SEQ],
                                            start=True, stop=True)
                last.then_inc(inner_full, 1)

            def weighted_values(bank, weights, a):
                for j in range(TT):
                    last = nc.tensor.matmul(ps[:, bank, P * j:SEQ], z_v[:, j, a, :],
                                            weights[:, COL_AT[j]:COL_AT[j] + SEQ - P * j],
                                            start=j == 0, stop=j == TT - 1)
                return last

            def ret_out(p):
                pe.wait_ge(z_done, N_RET + 5 * p + 5)
                pe.wait_ge(inner_ready, 2 * p + 2)
                for a in range(2):
                    weighted_values(4 + a, sm[a], a).then_inc(ret_full, 1)

            def ret_var(p):
                pe.wait_ge(sq_ready, p + 1)
                for a in range(2):
                    last = nc.tensor.matmul(ps[:, 4 + a, :], ones[:, :], z[:, a, :], start=True, stop=True)
                last.then_inc(var_full, 1)

            def ret_turn(p, prev):
                g, v = N_RET + 5 * p, V_RET + 40 * p
                tail = {1: [lambda: ret_out(p - 1)], 3: [lambda: ret_var(p - 1)]} if prev else {1: [iw_turn_over]}
                at_least(pe, inner_ready, 2 * p)
                if not prev:
                    pe.wait_ge(pt_ready, MEM_HEADS)
                    pe.wait_ge(sig_ready, 8)
                group(v, g, proj(6), tail, banks_free=False)
                group(v + 8, g + 1, proj(0), {5: [lambda: idx_scores(p, 0)], 7: [lambda: idx_scores(p, 1)]},
                      banks_free=True)
                at_least(pe, z_done, g)
                group(v + 16, g + 2, proj(2), {0: [lambda: idx_scores(p, 2)], 2: [lambda: idx_scores(p, 3)]},
                      banks_free=False)
                pe.wait_ge(z_done, g + 2)
                group(v + 24, g + 3, proj(0), {1: [lambda: inner(p, 0)], 4: [lambda: inner(p, 1)]})
                pe.wait_ge(z_done, g + 3)
                group(v + 32, g + 4, in_rows(2, h_hi, h_lo, TT, 2))

            ret_turn(0, False)
            with pe.Fori(1, NPAIR) as p:
                ret_turn(p, True)
            up_phase(V_UPR, N_UPR, 8, 12, 2, {1: [lambda: ret_out(3)], 3: [lambda: ret_var(3)]})

            def dsa_logits(p, a):
                pe.wait_ge(z_done, N_DSA + 4 * p + 2)
                at_least(pe, logit_read, MEM_HEADS + 2 * p + a)
                at_least(pe, pt_ready, MEM_HEADS + 2 * p)
                at_least(pe, y_done, 12 + 2 * p)
                for b in range(TT):
                    w = P * (b + 1)
                    last = nc.tensor.matmul(flat[:, PACKED + ROW_AT[b]:PACKED + ROW_AT[b] + w],
                                            z[:, 2 + a, P * b:P * b + P], z[:, a, 0:w], start=True, stop=True)
                last.then_inc(logit_full, 1)

            def dsa_turn_over(p, a):
                pe.wait_ge(p_ready, MEM_HEADS + 2 * p + a + 1)
                pe.wait_ge(pt_ready, MEM_HEADS + 2 * p + a)
                for j in range(TT):
                    for b in range(j, TT):
                        at = PACKED + COL_AT[j] + P * (b - j)
                        last = nc.tensor.transpose(flat[:, at:at + P],
                                                   pr[a][:, ROW_AT[b] + P * j:ROW_AT[b] + P * j + P], ident[:, :])
                last.then_inc(pt_full, 1)

            def dsa_out(p, a):
                pe.wait_ge(z_done, N_DSA + 4 * p + 4)
                pe.wait_ge(pt_ready, MEM_HEADS + 2 * p + 2)
                weighted_values((7, 4)[a], pt[a], a).then_inc(o_full, 1)

            def dsa_turn(p, prev):
                g, v = N_DSA + 4 * p, V_DSA + 32 * p
                tail = {1: [lambda: dsa_out(p - 1, 0)], 3: [lambda: dsa_out(p - 1, 1)]} if prev else {}
                if not prev:
                    pe.wait_ge(sig_ready, 16)
                group(v, g, proj(0), tail, banks_free=prev)
                group(v + 8, g + 1, proj(2))
                group(v + 16, g + 2, proj(0), {1: [lambda: dsa_logits(p, 0)], 4: [lambda: dsa_logits(p, 1)]})
                group(v + 24, g + 3, in_rows(2, h_hi, h_lo, TT, 2),
                      {2: [lambda: dsa_turn_over(p, 0)], 5: [lambda: dsa_turn_over(p, 1)]})

            dsa_turn(0, False)
            with pe.Fori(1, NPAIR) as p:
                dsa_turn(p, True)
            up_phase(V_UPD, N_UPD, 16, 20, 2, {1: [lambda: dsa_out(3, 0)], 3: [lambda: dsa_out(3, 1)]})

            pe.wait_ge(sig_ready, 24)
            for g in range(4):
                at_least(pe, out_done, 4 * (g - 1))
                if g == 1:
                    pe.wait_ge(z_done, N_OUT)

                def out_product(k, t):
                    wh, wl = [w[:, k % 4, :, :].rearrange("p a n -> p (a n)") for w in (w_hi, w_lo)]
                    dst, tok = ps[:, 4 * ((g + 1) % 2) + t, :], slice(P * t, P * t + P)
                    nc.tensor.matmul(dst, m_hi[:, k, tok], wh, start=k == 0, stop=False)
                    nc.tensor.matmul(dst, m_lo[:, k, tok], wh, start=False, stop=False)
                    return nc.tensor.matmul(dst, m_hi[:, k, tok], wl, start=False, stop=k == 15)

                by_half = 16 if g < 3 else 16 - LAST_HALVES
                for k in range(by_half):
                    pe.wait_ge(lo_ready, V_OUT + 16 * g + k + 1)
                    if g == 0:
                        pe.wait_ge(m_lo_done, k + 1)
                    for t in range(TT):
                        last = out_product(k, t)
                    last.then_inc(half_used, 1)
            pe.wait_ge(lo_ready, V_END)
            for t in range(TT):
                for k in range(by_half, 16):
                    last = out_product(k, t)
                last.then_inc(tile_whole, 1)

        @block.vector
        def _(dve):
            st = Steps(dve, own)
            V = nc.vector

            def rsqrt(a, y, u):
                st.then(V.tensor_scalar(u.bitcast(I32), a.bitcast(I32), 1, None, ALU.logical_shift_right))
                st.then(V.tensor_scalar(y.bitcast(I32), u.bitcast(I32), -1.0, RSQRT_SEED, ALU.mult, ALU.add))
                for _ in range(3):
                    st.then(V.scalar_tensor_tensor(out=u, in0=y, scalar=-0.5, in1=y, op0=ALU.mult, op1=ALU.mult))
                    st.then(V.tensor_tensor(u, u, a, ALU.mult))
                    st.then(V.scalar_tensor_tensor(out=y, in0=u, scalar=1.5, in1=y, op0=ALU.add, op1=ALU.mult))

            dve.wait_ge(norm_t, 1)
            V.tensor_copy(norm_w[:, 0:32], ps[:, 0, 0:32])
            V.tensor_scalar(norm_w[:, 32:40], ps[:, 0, 32:40], 0.25, None, ALU.mult).then_inc(norm_ready, 1)
            V.memset(stat[:, 1:3, :], 1.0)
            dve.wait_ge(consts, 11)
            V.tensor_scalar(negtri[:, :], iota_f[:, 0:P], 0.0, NEG, ALU.is_gt, ALU.mult)

            def square_sum(rows, col):
                V.tensor_tensor_reduce(out=junk[:, :], in0=rows, in1=rows, scale=1.0, scalar=0.0, op0=ALU.mult,
                                       op1=ALU.add, accum_out=stat[:, 0, col:col + 1]).then_inc(sq_rows, 1)

            def reciprocal_rms(c0, n):
                part = slice(c0, c0 + n)
                st.then(V.tensor_scalar(stat[:, 0, part], stat[:, 0, part], 1.0 / D, EPS, ALU.mult, ALU.add))
                rsqrt(stat[:, 0, part], stat[:, 1, part], stat[:, 2, part])

            def rows_lo(n):
                dve.wait_ge(t_hi, n + 1)
                k = n % KT
                hi_t, lo_t, bank, cols, col = ((memt_hi, memt_lo, 4 + k % 4, MEM, KT + k) if n < KT else
                                               (h_hi, h_lo, 4 + k % 4, SEQ, k))
                V.scalar_tensor_tensor(out=lo_t[:, k, :], in0=ps[:, bank, 0:cols], scalar=norm_w[:, col:col + 1],
                                       in1=hi_t[:, k, :].bitcast(F32), op0=ALU.mult,
                                       op1=ALU.subtract).then_inc(t_lo, 1)

            def take_km(g):
                dve.wait_ge(half_used, V_KV + 8 + 8 * g)
                V.tensor_tensor(km_f[:, :, :], ps[:, 2 * (g % 2):2 * (g % 2) + 2, 0:MEM],
                                rms_mem[:, :].unsqueeze(1).to_broadcast([P, 2, MEM]), ALU.mult).then_inc(z_done, 1)
                dve.wait_ge(z_done, g + 1)
                st.then(V.tensor_copy(km_hi[:, 2 * g:2 * g + 2, :], km_f[:, :, :]))
                st.then(V.tensor_tensor(km_lo[:, 2 * g:2 * g + 2, :], km_f[:, :, :],
                                        km_hi[:, 2 * g:2 * g + 2, :].bitcast(F32), ALU.subtract))

            def take_vm(i, e):
                dve.wait_ge(half_used, V_KV + 8 + 8 * e + 16 * i)
                for m in range(MT):
                    ins = V.tensor_scalar(vm[:, m, bass.ds(GC * 2 * (i - 2) + GC * e, GC)], ps[:, 2 * e + m, 0:GC],
                                          stat[:, 1, 4 + m:5 + m], 0.25, ALU.mult, ALU.mult)
                ins.then_inc(z_done, 1)

            for n in range(KT):
                rows_lo(n)
            for c in range(4):
                dve.wait_ge(mem_in[c], 16)
            for t in range(MT):
                at_least(dve, sq_rows, t)
                square_sum(mem_rows[:, t, :], 4 + t)
            dve.wait_ge(sq_rows, MT)
            reciprocal_rms(4, MT)
            for t in range(MT):
                ins = V.tensor_scalar(rms_diag[:, P * t:P * t + P], ident[:, :], stat[:, 1, 4 + t:5 + t], float(HD),
                                      ALU.mult, ALU.mult)
            ins.then_inc(diag_ready, 1)
            dve.wait_ge(rms_full, 1)
            st.then(V.tensor_copy(rms_mem[:, :], ps[:, 4, 0:MEM]))
            take_km(0)
            dve.wait_ge(x_in[TT - 1], 16)
            square_sum(x_rows[:, TT - 1, :], TT - 1)
            take_km(1)
            dve.wait_ge(sq_rows, MT + 1)
            dve.wait_ge(sq_done, TT - 1)
            reciprocal_rms(0, TT)
            for t in range(TT):
                V.tensor_scalar(x_rows[:, t, :], x_rows[:, t, :], stat[:, 1, t:t + 1], None,
                                ALU.mult).then_inc(row_scaled, 1)
            for n in range(KT):
                if X_OVER[n] >= 24 > X_OVER[n - 1]:
                    take_km(2)
                rows_lo(KT + n)
            take_km(3)
            with dve.Fori(2, 4) as i:
                take_vm(i, 0)
                take_vm(i, 1)

            def silu_gate(bank, tanhs):
                dve.wait_ge(tanh_done, tanhs)
                ins = V.scalar_tensor_tensor(out=z[:, 4:6, :], in0=z[:, 4:6, :], scalar=1.0,
                                             in1=ps[:, bank:bank + 2, :], op0=ALU.add, op1=ALU.mult)
                ins.then_inc(z_done, 1)
                st.then(V.tensor_copy(top8[:, 0:1], logg[:, 0:1]))

            def mem_finish(h):
                silu_gate(2, h + 1)
                values = vm[:, :, bass.ds(MEM_HD * h, MEM_HD)]
                st.then(V.tensor_copy(vh_hi[:, :, :], values))
                V.tensor_tensor(vh_lo[:, :, :], values, vh_hi[:, :, :].bitcast(F32), ALU.subtract)
                dve.wait_ge(pt_full, h + 1)
                st.then(V.tensor_copy(ptm_hi[:, :, :], ps[:, 6:8, :]))
                V.tensor_tensor(ptm_lo[:, :, :], ps[:, 6:8, :], ptm_hi[:, :, :].bitcast(F32),
                                ALU.subtract).then_inc(pt_ready, 1)
                dve.wait_ge(o_full, h + 1)
                write_y(2 * h, ps[:, 4:6, :], z[:, 4:6, :], z[:, 0:2, :], 1)

            def write_y(tile, a, b, tmp, signals):
                w = tmp.shape[1]
                dst_hi, dst_lo = y_hi[:, bass.ds(tile, w), :], y_lo[:, bass.ds(tile, w), :]
                st.then(V.tensor_tensor(tmp, a, b, ALU.mult))
                st.then(V.tensor_copy(dst_hi, tmp))
                V.tensor_tensor(dst_lo, tmp, dst_hi.bitcast(F32), ALU.subtract).then_inc(y_done, signals)

            def mem_turn(h, prev):
                if prev:
                    mem_finish(h - 1)
                dve.wait_ge(half_used, V_MEM + 8 + 16 * h)
                st.then(V.tensor_scalar(mq_hi[:, :, :], ps[:, 0:2, :], MEM_HD ** -0.5, None, ALU.mult))
                V.scalar_tensor_tensor(out=mq_lo[:, :, :], in0=ps[:, 0:2, :], scalar=MEM_HD ** -0.5,
                                       in1=mq_hi[:, :, :].bitcast(F32), op0=ALU.mult,
                                       op1=ALU.subtract).then_inc(z_done, 1)
                dve.wait_ge(logit_full, h + 1)
                st.then(V.tensor_copy(p_mem[:, :, :].rearrange("p t m -> p (t m)"), flat[:, 2048:3072]))
                V.tensor_reduce(rmax[:, 0, :], p_mem[:, :, :], AX.X, ALU.max, negate=True).then_inc(neg_max, 1)
                V.tensor_copy(top8[:, 0:1], logg[:, 0:1]).then_inc(logit_read, 1)
                dve.wait_ge(exp_done, h + 1)
                st.then(V.reciprocal(rinv[:, 0, :], rsum[:, 0, :]))
                for b in range(TT):
                    ins = V.tensor_scalar(p_mem[:, b, :], p_mem[:, b, :], rinv[:, 0, b:b + 1], None, ALU.mult)
                ins.then_inc(p_ready, 1)

            mem_turn(0, False)
            with dve.Fori(1, MEM_HEADS) as h:
                st.enter(h, 1, 8)
                mem_turn(h, True)
                st.leave(MEM_HEADS - 1, 8)

            def up_phase(v0, g0, sig0, first_branch, finish, extra=None, per=0, last_turn=None):
                def turn(i, first):
                    for e in range(2):
                        g = g0 + 4 * i + 2 * e
                        if first and e == 0:
                            finish()
                        if last_turn and isinstance(i, int) and i == 3 and e == 1:
                            last_turn()
                        dve.wait_ge(half_used, v0 + 12 + 12 * e + 24 * i)
                        dve.wait_ge(sig_ready, sig0 + 2 * i + e + 1)
                        tiles = merged[:, bass.ds(4 * i + 2 * e, 2), :]
                        if first_branch:
                            V.scalar_tensor_tensor(out=tiles, in0=z[:, 0:2, :], scalar=1.0, in1=ps[:, 2:4, :],
                                                   op0=ALU.add, op1=ALU.mult).then_inc(z_done, 2)
                        else:
                            st.then(V.scalar_tensor_tensor(out=z[:, 2:4, :], in0=z[:, 0:2, :], scalar=1.0,
                                                           in1=ps[:, 2:4, :], op0=ALU.add, op1=ALU.mult))
                            V.tensor_tensor(tiles, tiles, z[:, 2:4, :], ALU.add).then_inc(z_done, 2)
                        if extra:
                            extra(i, e)
                turn(0, True)
                if last_turn:
                    with dve.Fori(1, 3) as i:
                        st.enter(i, 1, per)
                        turn(i, False)
                        st.leave(2, per)
                    turn(3, False)
                    return
                if extra:
                    for i in range(1, 4):
                        turn(i, False)
                    return
                with dve.Fori(1, 4) as i:
                    st.enter(i, 1, per)
                    turn(i, False)
                    st.leave(3, per)

            up_phase(V_UPM, N_UPM, 0, True, lambda: mem_finish(3))

            dve.wait_ge(half_used, V_IKW + 8)
            ik_psum = ps[0:IDX_DIM, 5, :]
            V.tensor_copy(ik_hi[0:IDX_DIM, :], ik_psum)
            st.then(V.tensor_copy(ik_hi[IDX_DIM:P, :], ik_psum))
            for half in (slice(0, IDX_DIM), slice(IDX_DIM, P)):
                V.tensor_tensor(ik_lo[half, :], ik_psum, ik_hi[0:IDX_DIM, :].bitcast(F32), ALU.subtract)
            V.tensor_scalar(iwt[:, :], ps[IDX_DIM:IKW, 5, :], (IDX_HEADS ** -0.5) * (IDX_DIM ** -0.5), None,
                            ALU.mult).then_inc(iwt_ready, 1)
            V.memset(score[:, :], 0.0).then_inc(z_done, 1)
            dve.wait_ge(iwt_full, 1)
            V.tensor_copy(iw[:, :, :].rearrange("p t h -> p (t h)"),
                          ps[:, 4, 0:TT * IDX_HEADS]).then_inc(iw_ready, 1)

            def ret_finish(p):
                o, a, y, u = z[:, 2:4, :], z[:, 0:2, :], z[:, 6:8, :], scratch[:, :, :]
                dve.wait_ge(ret_full, 2 * p + 2)
                st.then(V.tensor_copy(o, ps[:, 4:6, :]))
                V.tensor_tensor(a, o, o, ALU.mult).then_inc(sq_ready, 1)
                dve.wait_ge(var_full, p + 1)
                V.tensor_scalar(a, ps[:, 4:6, :], GN_EPS, None, ALU.add).then_inc(var_read, 1)
                st.then(V.tensor_copy(top8[:, 0:1], logg[:, 0:1]))
                rsqrt(a, y, u)
                for b in range(2):
                    ins = V.scalar_tensor_tensor(out=o[:, b, :], in0=o[:, b, :],
                                                 scalar=norm_w[:, bass.ds(2 * KT + 2 * p + b, 1)],
                                                 in1=y[:, b, :], op0=ALU.mult, op1=ALU.mult)
                st.then(ins)
                write_y(2 * p, o, z[:, 4:6, :], a, 2)

            def ret_turn(p, prev):
                g = N_RET + 5 * p
                if prev:
                    ret_finish(p - 1)
                dve.wait_ge(half_used, V_RET + 8 + 40 * p)
                for n in range(4):
                    src = ps[IDX_DIM * (n % 2):IDX_DIM * (n % 2) + IDX_DIM, 6 + n // 2, :]
                    ins = V.tensor_copy(iq[n // 2][0:IDX_DIM, n % 2, :], src)
                st.then(ins)
                for n in range(4):
                    src = ps[IDX_DIM * (n % 2):IDX_DIM * (n % 2) + IDX_DIM, 6 + n // 2, :]
                    ins = V.tensor_tensor(iq[n // 2][IDX_DIM:P, n % 2, :], src,
                                          iq[n // 2][0:IDX_DIM, n % 2, :].bitcast(F32), ALU.subtract)
                ins.then_inc(z_done, 1)
                dve.wait_ge(half_used, V_RET + 16 + 40 * p)
                V.tensor_scalar(z[:, 0:2, :], ps[:, 0:2, :], HD ** -0.5, None, ALU.mult).then_inc(z_done, 1)
                for n in range(4):
                    dve.wait_ge(relu_done, 4 * p + n + 1)
                    for b in range(TT):
                        w = P * (b + 1)
                        part = slice(ROW_AT[b], ROW_AT[b] + w)
                        ins = V.scalar_tensor_tensor(out=score[:, part], in0=sm[n % 2][:, part],
                                                     scalar=iw[:, b, bass.ds(4 * p + n, 1)], in1=score[:, part],
                                                     op0=ALU.mult, op1=ALU.add)
                    ins.then_inc(relu_used, 1)
                    if n == 3:
                        dve.wait_ge(half_used, V_RET + 24 + 40 * p)
                        V.tensor_copy(z[:, 2:4, :], ps[:, 2:4, :]).then_inc(z_done, 1)
                    dve.wait_ge(relu_used, 4 * p + n + 1)
                for a in range(2):
                    dve.wait_ge(decay_ready, 2 * p + a + 1)
                    st.then(V.scalar_tensor_tensor(out=decay[:, 0:P], in0=iota_f[:, 0:P], scalar=0.0,
                                                   in1=decay[:, 0:P], op0=ALU.is_ge, op1=ALU.mult))
                    dve.wait_ge(inner_full, 2 * p + a + 1)
                    for j in range(TT):
                        w = SEQ - P * j
                        at = COL_AT[j]
                        ins = V.tensor_tensor(sm[a][:, at:at + w], flat[:, PACKED + at:PACKED + at + w],
                                              decay[:, 0:w], ALU.mult)
                    ins.then_inc(inner_ready, 1)
                silu_gate(0, MEM_HEADS + p + 1)
                dve.wait_ge(half_used, V_RET + 40 + 40 * p)
                rows = flat[:, 1024:2048].rearrange("p (t h d) -> p (t h) d", h=2, d=HD)
                st.then(V.tensor_reduce(stat[:, 0, :], rows, AX.X, ALU.add))
                st.then(V.tensor_scalar(stat[:, 0, :], stat[:, 0, :], 1.0 / HD, None, ALU.mult))
                V.tensor_tensor(z_v.rearrange("p t h d -> p (t h) d"), rows,
                                stat[:, 0, :].unsqueeze(2).to_broadcast([P, 8, HD]),
                                ALU.subtract).then_inc(z_done, 1)

            RET_STEPS = 22
            ret_turn(0, False)
            with dve.Fori(1, NPAIR) as p:
                st.enter(p, 1, RET_STEPS)
                ret_turn(p, True)
                st.leave(NPAIR - 1, RET_STEPS)

            def select_keys(b, e):
                w = P * (b + 1)
                part = slice(ROW_AT[b], ROW_AT[b] + w)
                row = score[:, part]
                if w > TOPK:
                    if e == 0:
                        st.then(V.tensor_copy(top8[:, 0:1], logg[:, 0:1]))
                    for _ in range(TOPK // 16):
                        st.then(V.max(out=top8[:, :], in_=row))
                        st.then(V.match_replace(out=row, in_to_replace=top8[:, :], in_values=row, imm_value=TAKEN))
                if e == 1:
                    if w > TOPK:
                        st.then(V.tensor_scalar(row, row, TAKEN / 2, FAR, ALU.is_gt, ALU.mult))
                    else:
                        st.then(V.memset(row, 0.0))
                    st.then(V.tensor_tensor(row, row, iota_f[:, 0:w], ALU.subtract))
                    st.then(V.tensor_scalar(far[:, part], row, float(P * b), None, ALU.add))

            def ret_end():
                ret_finish(3)
                for b in range(TT):
                    d = score[:, ROW_AT[b] + P * b:ROW_AT[b] + P * b + P]
                    V.tensor_tensor(d, d, negtri[:, :], ALU.add)

            up_phase(V_UPR, N_UPR, 8, False, ret_end, select_keys)
            for b in range(TT):
                d = far[:, ROW_AT[b] + P * b:ROW_AT[b] + P * b + P]
                st.then(V.scalar_tensor_tensor(out=d, in0=negtri[:, :], scalar=FAR / NEG, in1=d,
                                               op0=ALU.mult, op1=ALU.add))

            def dsa_finish(p):
                for a in range(2):
                    dve.wait_ge(o_full, MEM_HEADS + 2 * p + a + 1)
                    write_y(2 * p + a, ps[:, (7, 4)[a]:(7, 4)[a] + 1, :], z[:, 4 + a:5 + a, :], z[:, 3:4, :], 1)
                    st.then(V.tensor_copy(top8[:, 0:1], logg[:, 0:1]))

            def dsa_turn(p, prev):
                g = N_DSA + 4 * p
                if prev:
                    dsa_finish(p - 1)
                dve.wait_ge(half_used, V_DSA + 8 + 32 * p)
                V.tensor_scalar(z[:, 0:2, :], ps[:, 0:2, :], HD ** -0.5, None, ALU.mult).then_inc(z_done, 1)
                dve.wait_ge(half_used, V_DSA + 16 + 32 * p)
                V.tensor_copy(z[:, 2:4, :], ps[:, 2:4, :]).then_inc(z_done, 1)
                for a in range(2):
                    dve.wait_ge(logit_full, MEM_HEADS + 2 * p + a + 1)
                    for b in range(TT):
                        w, at = P * (b + 1), ROW_AT[b]
                        ins = V.scalar_tensor_tensor(out=pr[a][:, at:at + w], in0=far[:, at:at + w],
                                                     scalar=slope[:, bass.ds(2 * p + a, 1)],
                                                     in1=flat[:, PACKED + at:PACKED + at + w],
                                                     op0=ALU.mult, op1=ALU.add)
                    ins.then_inc(logit_read, 1)
                    dve.wait_ge(logit_read, MEM_HEADS + 2 * p + a + 1)
                    for b in range(TT):
                        w, at = P * (b + 1), ROW_AT[b]
                        ins = V.tensor_reduce(rmax[:, a, b:b + 1], pr[a][:, at:at + w], AX.X, ALU.max, negate=True)
                    ins.then_inc(neg_max, 1)
                for a in range(2):
                    dve.wait_ge(exp_done, MEM_HEADS + 2 * p + a + 1)
                    st.then(V.reciprocal(rinv[:, a, :], rsum[:, a, :]))
                    for b in range(TT):
                        w, at = P * (b + 1), ROW_AT[b]
                        ins = V.tensor_scalar(pr[a][:, at:at + w], pr[a][:, at:at + w], rinv[:, a, b:b + 1], None,
                                              ALU.mult)
                    ins.then_inc(p_ready, 1)
                for a in range(2):
                    dve.wait_ge(pt_full, MEM_HEADS + 2 * p + a + 1)
                    V.tensor_copy(pt[a][:, :], flat[:, PACKED:PACKED + PACK]).then_inc(pt_ready, 1)
                    if a == 0:
                        silu_gate(0, MEM_HEADS + NPAIR + p + 1)
                dve.wait_ge(half_used, V_DSA + 32 + 32 * p)
                V.tensor_scalar(z_v.rearrange("p t h d -> p (t h d)"), flat[:, 1024:2048], 0.25, None,
                                ALU.mult).then_inc(z_done, 1)

            DSA_STEPS = 9
            dsa_turn(0, False)
            with dve.Fori(1, NPAIR) as p:
                st.enter(p, 1, DSA_STEPS)
                dsa_turn(p, True)
                st.leave(NPAIR - 1, DSA_STEPS)

            def merged_lo(k):
                dve.wait_ge(m_hi_done, k + 1)
                V.tensor_tensor(m_lo[:, k, :], merged[:, k, :], m_hi[:, k, :].bitcast(F32),
                                ALU.subtract).then_inc(m_lo_done, 1)

            up_phase(V_UPD, N_UPD, 16, False, lambda: dsa_finish(3), None, 2,
                     lambda: [merged_lo(k) for k in range(KT // 4)])
            for k in range(KT // 4, KT):
                merged_lo(k)
            dve.wait_ge(post_in, 16)
            for g in range(4):
                for t in range(TT):
                    dve.wait_ge(out_sq, 4 * g + t + 1)
                    V.tensor_tensor(o_rows[:, t, 512 * g:512 * g + 512], ps[:, 4 * ((g + 1) % 2) + t, :],
                                    post_w[:, 512 * g:512 * g + 512], ALU.mult).then_inc(out_done, 1)
            st.then(V.tensor_reduce(stat[:, 0, 0:TT], ssq[:, :, :], AX.X, ALU.add))
            st.then(V.tensor_scalar(stat[:, 0, 0:TT], stat[:, 0, 0:TT], 1.0 / D, EPS, ALU.mult, ALU.add))
            rsqrt(stat[:, 0, 0:TT], stat[:, 1, 0:TT], stat[:, 2, 0:TT])
            V.tensor_copy(top8[:, 0:1], stat[:, 1, 0:1]).then_inc(rstd_ready, 1)
            dve.wait_ge(again_in, 16 * TT)
            for t in range(TT - 1):
                for c in (slice(0, D // 2), slice(D // 2, D)):
                    V.scalar_tensor_tensor(out=o_rows[:, t, c], in0=o_rows[:, t, c], scalar=stat[:, 1, t:t + 1],
                                           in1=x_again[:, t, c], op0=ALU.mult, op1=ALU.add).then_inc(final, 1)


_INS = ["x", "mem", "pre_norm_w", "w_in", "ret_gn_w", "mem_norm_w", "w_mem_kv", "w_up_ret", "w_up_dsa",
        "w_up_mem", "w_o", "post_norm_w"]


def kernel(**inputs):
    import numpy as _np
    import concourse.bacc as _bacc
    from concourse import mybir as _mybir
    from concourse.bass_utils import run_bass_kernel_spmd as _run

    nc = _bacc.Bacc("TRN2", target_bir_lowering=False, num_devices=1)
    arrays, args = {}, []
    for name in _INS:
        a = _np.ascontiguousarray(inputs[name])
        arrays[f"in_{name}"] = a
        args.append(nc.dram_tensor(f"in_{name}", a.shape, _mybir.dt.from_np(a.dtype), kind="ExternalInput").ap())
    args.append(nc.dram_tensor("out_0", (1, SEQ, D), F32, kind="ExternalOutput").ap())
    build(nc, *args)
    r = _run(nc, [arrays], core_ids=[0])
    return r.results[0]["out_0"]
```
